# Optimizing a Trainium2 kernel written in Bass

```python
import math
import jax, jax.numpy as jnp
from jax import lax
import numpy as np

D_MODEL = 1024
BATCH = 1
SEQ = 1024
DEPTH = 1
DEC_BATCH = 8
DEC_SEQ = 8
PAST_LEN = 4096
PAGE_SIZE = 128

D_MIX = D_MODEL
ATT_HEADS = 8
ATT_KV_HEADS = 2
ATT_HEAD_DIM = 64
ATT_GROUP = ATT_HEADS // ATT_KV_HEADS
ATT_WIDTH = ATT_HEADS * ATT_HEAD_DIM
KV_WIDTH = ATT_KV_HEADS * ATT_HEAD_DIM
WINDOW = 128
M_HEADS = 4
M_HEAD_DIM = (D_MIX - ATT_WIDTH) // M_HEADS
M_WIDTH = M_HEADS * M_HEAD_DIM
M_CHUNK = 128
NORM_EPS = 1e-6
NEG_BIG = -1e30

SPLIT_SIZES = (ATT_WIDTH, KV_WIDTH, KV_WIDTH, ATT_WIDTH,
               M_WIDTH, M_WIDTH, M_WIDTH, M_WIDTH, M_WIDTH,
               M_HEADS, M_HEADS)
D_IN = sum(SPLIT_SIZES)
SPLIT_POINTS = tuple(int(s) for s in np.cumsum(SPLIT_SIZES)[:-1])

kernel_name = "hymba_mlstm_swa_sink_alibi_step"

def _rms(x, g):
    xf = x.astype(jnp.float32)
    y = xf * lax.rsqrt(jnp.mean(xf * xf, axis=-1, keepdims=True) + NORM_EPS)
    return (y * g.astype(jnp.float32)).astype(x.dtype)

def _alibi_slopes():
    s = 2.0 ** (-8.0 * (np.arange(ATT_HEADS) + 1) / ATT_HEADS)
    return jnp.asarray(s.astype(np.float32)).reshape(ATT_KV_HEADS, ATT_GROUP)

def _alibi_window_bias(diff, key_ok):
    valid = (diff >= 0) & (diff < WINDOW) & key_ok
    slopes = _alibi_slopes()[:, :, None, None]
    pen = -slopes * diff[..., None, None, :, :].astype(jnp.float32)
    return jnp.where(valid[..., None, None, :, :], pen, NEG_BIG)

def _sink_attention(q, k, v, bias, sinks):
    s = jnp.einsum('...qhgd,...khd->...hgqk', q, k).astype(jnp.float32) * (ATT_HEAD_DIM ** -0.5) + bias
    sink = jnp.broadcast_to(sinks.astype(jnp.float32)[:, :, None, None], s.shape[:-1] + (1,))
    p = jax.nn.softmax(jnp.concatenate([s, sink], axis=-1), axis=-1)[..., :-1]
    return jnp.einsum('...hgqk,...khd->...qhgd', p.astype(v.dtype), v)

def _attend_prompt(q, k, v, sinks):
    B, T = q.shape[:2]
    nb = T // WINDOW
    qb = q.reshape(B, nb, WINDOW, ATT_KV_HEADS, ATT_GROUP, ATT_HEAD_DIM)
    pad = jnp.zeros((B, WINDOW, ATT_KV_HEADS, ATT_HEAD_DIM), k.dtype)
    kp = jnp.concatenate([pad, k], axis=1).reshape(B, nb + 1, WINDOW, ATT_KV_HEADS, ATT_HEAD_DIM)
    vp = jnp.concatenate([pad, v], axis=1).reshape(B, nb + 1, WINDOW, ATT_KV_HEADS, ATT_HEAD_DIM)
    kb = jnp.concatenate([kp[:, :-1], kp[:, 1:]], axis=2)
    vb = jnp.concatenate([vp[:, :-1], vp[:, 1:]], axis=2)
    blk = jnp.arange(nb)
    qpos = blk[:, None] * WINDOW + jnp.arange(WINDOW)[None, :]
    kpos = (blk[:, None] - 1) * WINDOW + jnp.arange(2 * WINDOW)[None, :]
    diff = qpos[:, :, None] - kpos[:, None, :]
    bias = _alibi_window_bias(diff, (kpos >= 0)[:, None, :])
    out = _sink_attention(qb, kb, vb, bias, sinks)
    return out.reshape(B, T, ATT_WIDTH), k[:, -WINDOW:], v[:, -WINDOW:]

def _attend_sample(q, k, v, sinks, win_k, win_v):
    B, T = q.shape[:2]
    k_all = jnp.concatenate([win_k.astype(k.dtype), k], axis=1)
    v_all = jnp.concatenate([win_v.astype(v.dtype), v], axis=1)
    qpos = jnp.arange(T)
    kpos = jnp.concatenate([jnp.arange(WINDOW) - WINDOW, jnp.arange(T)])
    diff = qpos[:, None] - kpos[None, :]
    bias = _alibi_window_bias(diff, True)
    out = _sink_attention(q, k_all, v_all, bias, sinks)
    return out.reshape(B, T, ATT_WIDTH), k_all[:, -WINDOW:], v_all[:, -WINDOW:]

def _chunk_len(T):
    return T if T <= M_CHUNK else math.gcd(T, M_CHUNK)

def _mlstm(q, k, v, i_pre, logf, C0, n0, m0):
    B, T = q.shape[:2]
    L = _chunk_len(T)
    nc = T // L

    def to_chunks(a):
        a = a.astype(jnp.float32).reshape((B, nc, L) + a.shape[2:])
        a = jnp.moveaxis(a, 3, 2)
        return jnp.moveaxis(a, 1, 0)

    causal = jnp.tril(jnp.ones((L, L), dtype=bool))

    def step(carry, xs):
        C, n, m = carry
        qc, kc, vc, ic, fc = xs
        b = jnp.cumsum(fc, axis=-1)
        m_intra = b + lax.cummax(ic - b, axis=ic.ndim - 1)
        m_t = jnp.maximum(b + m[..., None], m_intra)
        logD = b[..., :, None] - b[..., None, :] + ic[..., None, :] - m_t[..., :, None]
        Dm = jnp.exp(jnp.where(causal, logD, -jnp.inf))
        S = jnp.einsum('bhtd,bhsd->bhts', qc, kc) * Dm
        g = jnp.exp(b + m[..., None] - m_t)
        num = jnp.einsum('bhts,bhsv->bhtv', S, vc) + g[..., None] * jnp.einsum('bhtd,bhdv->bhtv', qc, C)
        den = jnp.sum(S, axis=-1) + g * jnp.einsum('bhtd,bhd->bht', qc, n)
        h = num / jnp.maximum(jnp.abs(den), jnp.exp(-m_t))[..., None]
        m_new = m_t[..., -1]
        w = jnp.exp(b[..., -1:] - b + ic - m_new[..., None])
        decay = jnp.exp(b[..., -1] + m - m_new)
        C_new = decay[..., None, None] * C + jnp.einsum('bhs,bhsd,bhsv->bhdv', w, kc, vc)
        n_new = decay[..., None] * n + jnp.einsum('bhs,bhsd->bhd', w, kc)
        return (C_new, n_new, m_new), h

    init = (C0.astype(jnp.float32), n0.astype(jnp.float32), m0.astype(jnp.float32))
    xs = (to_chunks(q), to_chunks(k), to_chunks(v), to_chunks(i_pre), to_chunks(logf))
    (C, n, m), h = lax.scan(step, init, xs)
    h = jnp.moveaxis(jnp.moveaxis(h, 0, 1), 2, 3).reshape(B, T, M_HEADS, M_HEAD_DIM)
    return h, C, n, m

def _layer(x, g_pre, w_in, b_gate, sinks, g_mh, w_out, g_post, attend, C0, n0, m0):
    B, T, _ = x.shape
    xn = _rms(x, g_pre)
    proj = xn @ w_in
    qa, ka, va, za, qm, km, vm, om, zm, ig, fg = jnp.split(proj, SPLIT_POINTS, axis=-1)
    qa = qa.reshape(B, T, ATT_KV_HEADS, ATT_GROUP, ATT_HEAD_DIM)
    ka = ka.reshape(B, T, ATT_KV_HEADS, ATT_HEAD_DIM)
    va = va.reshape(B, T, ATT_KV_HEADS, ATT_HEAD_DIM)
    att, wk, wv = attend(qa, ka, va, sinks.reshape(ATT_KV_HEADS, ATT_GROUP))
    a_out = att * jax.nn.silu(za)
    bg = b_gate.astype(jnp.float32)
    i_pre = ig.astype(jnp.float32) + bg[:M_HEADS]
    logf = jax.nn.log_sigmoid(fg.astype(jnp.float32) + bg[M_HEADS:])
    h, C, n, m = _mlstm(qm.reshape(B, T, M_HEADS, M_HEAD_DIM),
                        km.reshape(B, T, M_HEADS, M_HEAD_DIM) * (M_HEAD_DIM ** -0.5),
                        vm.reshape(B, T, M_HEADS, M_HEAD_DIM), i_pre, logf, C0, n0, m0)
    h = _rms(h, g_mh).astype(x.dtype).reshape(B, T, M_WIDTH)
    m_out = jax.nn.sigmoid(om) * h * jax.nn.silu(zm)
    y = jnp.concatenate([a_out, m_out], axis=-1) @ w_out
    return x + _rms(y, g_post), (wk, wv, C, n, m)

def setup_inputs(seed: int = 0) -> dict:
    key = jax.random.key(seed)
    ks = jax.random.split(key, 20)
    f32 = jnp.float32
    x_prompt = jax.random.normal(ks[0], (BATCH, SEQ, D_MODEL), f32)
    x_sample = jax.random.normal(ks[1], (DEC_BATCH, DEC_SEQ, D_MODEL), f32)
    cache_win_k = jax.random.normal(ks[2], (DEPTH, DEC_BATCH, WINDOW, ATT_KV_HEADS, ATT_HEAD_DIM), f32)
    cache_win_v = jax.random.normal(ks[3], (DEPTH, DEC_BATCH, WINDOW, ATT_KV_HEADS, ATT_HEAD_DIM), f32)
    state_C = 0.5 * jax.random.normal(ks[4], (DEPTH, DEC_BATCH, M_HEADS, M_HEAD_DIM, M_HEAD_DIM), f32)
    state_n = jax.random.normal(ks[5], (DEPTH, DEC_BATCH, M_HEADS, M_HEAD_DIM), f32)
    state_m = jax.random.normal(ks[6], (DEPTH, DEC_BATCH, M_HEADS), f32)
    g_pre = 1.0 + 0.05 * jax.random.normal(ks[7], (DEPTH, D_MODEL), f32)
    w_in = jax.random.normal(ks[8], (DEPTH, D_MODEL, D_IN), f32) * (D_MODEL ** -0.5)
    b_i = 0.1 * jax.random.normal(ks[9], (DEPTH, M_HEADS), f32)
    b_f = jnp.linspace(3.0, 6.0, M_HEADS, dtype=f32)[None, :] + 0.1 * jax.random.normal(ks[10], (DEPTH, M_HEADS), f32)
    b_gate = jnp.concatenate([b_i, b_f], axis=-1)
    attn_sinks = 0.5 * jax.random.normal(ks[11], (DEPTH, ATT_HEADS), f32)
    g_mh = 1.0 + 0.05 * jax.random.normal(ks[12], (DEPTH, M_HEADS, M_HEAD_DIM), f32)
    w_out = jax.random.normal(ks[13], (DEPTH, D_MIX, D_MODEL), f32) * (D_MIX ** -0.5)
    g_post = 1.0 + 0.05 * jax.random.normal(ks[14], (DEPTH, D_MODEL), f32)
    return {"x_prompt": x_prompt, "x_sample": x_sample,
            "cache_win_k": cache_win_k, "cache_win_v": cache_win_v,
            "state_C": state_C, "state_n": state_n, "state_m": state_m,
            "g_pre": g_pre, "w_in": w_in, "b_gate": b_gate, "attn_sinks": attn_sinks,
            "g_mh": g_mh, "w_out": w_out, "g_post": g_post}

def reference(x_prompt, x_sample, cache_win_k, cache_win_v, state_C, state_n, state_m,
              g_pre, w_in, b_gate, attn_sinks, g_mh, w_out, g_post):
    yp, ys = x_prompt, x_sample
    Bp = x_prompt.shape[0]
    p_states = ([], [], [], [], [])
    s_states = ([], [], [], [], [])
    for l in range(DEPTH):
        C0 = jnp.zeros((Bp, M_HEADS, M_HEAD_DIM, M_HEAD_DIM), jnp.float32)
        n0 = jnp.zeros((Bp, M_HEADS, M_HEAD_DIM), jnp.float32)
        m0 = jnp.zeros((Bp, M_HEADS), jnp.float32)
        yp, st_p = _layer(yp, g_pre[l], w_in[l], b_gate[l], attn_sinks[l], g_mh[l], w_out[l], g_post[l],
                          _attend_prompt, C0, n0, m0)
        wk_l, wv_l = cache_win_k[l], cache_win_v[l]
        attend_s = lambda q, k, v, s, wk=wk_l, wv=wv_l: _attend_sample(q, k, v, s, wk, wv)
        ys, st_s = _layer(ys, g_pre[l], w_in[l], b_gate[l], attn_sinks[l], g_mh[l], w_out[l], g_post[l],
                          attend_s, state_C[l], state_n[l], state_m[l])
        for lst, a in zip(p_states, st_p):
            lst.append(a)
        for lst, a in zip(s_states, st_s):
            lst.append(a)
    wk_p, wv_p, C_p, n_p, m_p = [jnp.stack(a, axis=0) for a in p_states]
    wk_s, wv_s, C_s, n_s, m_s = [jnp.stack(a, axis=0) for a in s_states]
    return (yp, ys, wk_p, wv_p, C_p, n_p, m_p, wk_s, wv_s, C_s, n_s, m_s)


_drawn_inputs = setup_inputs


def setup_inputs(seed=0):
    import zlib

    import numpy as np

    out = dict(_drawn_inputs(seed))
    spreads = {}
    factors = {}
    for name, (base, spread) in spreads.items():
        noise = np.random.default_rng([zlib.crc32(name.encode()), seed]).standard_normal(out[name].shape)
        drawn = base * np.exp(spread * noise) if base else spread * noise
        out[name] = __import__('jax').numpy.asarray(drawn.astype(out[name].dtype))
    for name, factor in factors.items():
        out[name] = (out[name] * factor).astype(out[name].dtype)
    return out
```

```python
import numpy as np
import concourse.bass as bass
from concourse import mybir

F32 = mybir.dt.float32
F32R = mybir.dt.float32r
BF16 = mybir.dt.bfloat16
ALU = mybir.AluOpType
ACT = mybir.ActivationFunctionType
AX_X = mybir.AxisListType.X

P = 128
D = 1024
KT = D // P
T_P, DEC_B, DEC_T = 1024, 8, 8
T_S = DEC_B * DEC_T
T = T_P + T_S
NC = T_P // P
NTILE = NC + 1
AH, KVH, HD = 8, 2, 64
G = AH // KVH
WIN = 128
MH, MD = 4, 128
EPS = 1e-6
NEG = -1e30
PQ = 32
A_W, KV_W, M_W = AH * HD, KVH * HD, MH * MD
KEYS_S = WIN + DEC_T
W1 = MD + 1

C_QA, C_KA = 0, A_W
C_VA = C_KA + KV_W
C_ZA = C_VA + KV_W
C_QM = C_ZA + A_W
C_KM, C_VM, C_OM, C_ZM = (C_QM + i * M_W for i in range(1, 5))
C_G = C_ZM + M_W

SUBS = [(0, 364), (364, 364), (728, 360)]
TILES = ["ka"] + ["qa"] * 4 + ["km"] * 4 + ["qm"] * 4 + ["za"] * 4 + ["om"] * 4 + ["zm"] * 4
FIRST = {"ka": 0, "qa": 1, "km": 5, "qm": 9, "za": 13, "om": 17, "zm": 21}
NJ = len(TILES)
NSUB = 3 * NJ
S_P2, S_P3, S_P4 = 3 * FIRST["km"], 3 * FIRST["za"], 3 * FIRST["om"]
TOK_W = 648
TOK_H = TOK_W // 2
VA0 = TOK_H - 2 * MD


def weight_sequence():
    seq = []
    for j in range(NJ):
        seq.append(("in", j))
        if j >= NJ - 4:
            seq.append(("out", j - (NJ - 4)))
    return seq + [("out", k) for k in range(4, KT)]


SEQ = weight_sequence()
POS = {item: n for n, item in enumerate(SEQ)}


def split_plan():
    plan = {-1: [POS[("in", 0)]]}
    for j in range(NJ - 1):
        plan.setdefault(3 * j, []).append(POS[("in", j + 1)])
    for k in range(4):
        plan[3 * (NJ - 5 + k) + 2] = [POS[("out", k)]]
    return plan


PLAN = split_plan()


def build(nc, i, o):
    base = 16512
    XW = KT * T + T_S
    CW = MH * T + T_S
    sizes = [("A", 2 * 4 * XW), ("H", 6 * 4096), ("K", 2816), ("B", 16 * T), ("E", 4 * NTILE * MH * W1),
             ("D", 16 * T), ("C", 16 * T), ("F", 16 * T), ("GI", 27072)]
    off, at = base, {}
    for name, size in sizes:
        at[name] = off
        off += (size + 31) // 32 * 32
    end = off

    def sb(name, shape, dt, offset):
        return nc.alloc_sbuf_tensor_at(name, shape, dt, offset=offset)

    A, H, B, C, Dr, E, Fr, GI = (at[k] for k in ("A", "H", "B", "C", "D", "E", "F", "GI"))
    xh = sb("xh", [P, XW], F32R, A)
    xl = sb("xl", [P, XW], F32R, A + 4 * XW)
    w_raw = sb("w_raw", [P, 2, 1024], F32, H)
    w_hi = sb("w_hi", [P, 2, 1024], F32R, H + 8192)
    w_lo = sb("w_lo", [P, 2, 1024], F32R, H + 16384)
    qaT = sb("qaT", [P, G, T], F32, B)
    vm1 = sb("vm1", [P, NTILE, MH, W1], F32, E)
    kmT = sb("kmT", [P, MH, T], F32, Dr)
    qmT = sb("qmT", [P, MH, T], F32, C)
    zaT = sb("zaT", [P, G, T], F32, Fr)
    kaT = sb("kaT", [P, T], F32, GI)
    va = sb("va", [P, NTILE, KV_W], F32, GI + 4352)
    k = [at["K"]]

    def small(name, shape, dt=F32):
        n = int(np.prod(shape[1:])) * (2 if dt == BF16 else 4)
        t = sb(name, shape, dt, k[0])
        k[0] += (n + 31) // 32 * 32
        assert k[0] <= at["B"], (name, k[0] - at["B"])
        return t

    ident = small("ident", [P, P])
    ident_b = small("ident_b", [P, P], BF16)
    mask_b = small("mask_b", [P, P], BF16)
    seqmask_b = small("seqmask_b", [T_S, T_S], BF16)
    r1c = small("r1c", [P, NTILE, MH])
    r2c = small("r2c", [P, NTILE, MH])
    enm = small("enm", [P, NTILE, MH])
    glc = small("glc", [T_S, MH])
    mpb = small("mpb", [P, NC, MH])
    dec_s = small("dec_s", [P, DEC_B, MH])
    n_s = small("n_s", [P, DEC_B, MH])
    gmh = small("gmh", [P, MH])
    sink_p = small("sink_p", [P, AH])
    sink_s = small("sink_s", [P, 4])
    seqsel = small("seqsel", [T_S, DEC_B])
    newmask = small("newmask", [P, 2, DEC_B])
    stat = small("stat", [P, 2 * NTILE])
    half = small("half", [P, 4])
    ones = small("ones", [P, 1])
    x_raw = sb("x_raw", [P, 4, D], F32, B)
    wt_raw = sb("wt_raw", [P, KT, TOK_W], F32, H)
    wt_hi = sb("wt_hi", [P, KT, TOK_W], F32R, Dr)
    wt_lo = sb("wt_lo", [P, KT, TOK_W], F32R, Dr + 4 * KT * TOK_W)
    g_pre_b = sb("g_pre_b", [P, D], F32, Dr + 8 * KT * TOK_W)
    junk = sb("junk", [P, D], F32, Dr + 8 * KT * TOK_W + 4096)
    gates = sb("gates", [P, NTILE, 2 * PQ], F32, GI + 9984)
    masks32 = sb("masks32", [P, 2, P], F32, GI + 8960)
    row = [sb(f"row{n}", [MH, T], F32, Dr + n * 4 * T) for n in range(6)]
    ib, fb, ra, rb, rc, rd = row
    NR = 3 * PQ + MH
    rows = sb("rows", [NR, T], F32, Dr + 6 * 4 * T)
    re_, rf, r_m, r_gl = (rows[q * PQ:q * PQ + MH, :] for q in range(4))
    P1S = Dr + 8 * KT * TOK_W + 8192
    resets = sb("resets", [MH, T], F32, Fr)
    bgi = sb("bgi", [MH, 1], F32, P1S)
    bgf = sb("bgf", [PQ + MH, 1], F32, P1S + 32)
    m0T = sb("m0T", [MH, DEC_B], F32, P1S + 64)
    mp = sb("mp", [MH, NC + DEC_B], F32, P1S + 128)
    m_last = sb("m_last", [MH, 1 + DEC_B], F32, P1S + 384)
    mpd = sb("mpd", [MH, NC, MH], F32, P1S + 256)
    bias_p = sb("bias_p", [P, AH, 2 * WIN], F32, GI + 17408)
    bias_s = sb("bias_s", [P, KVH, KEYS_S], F32, GI + 25600)
    kcT = sb("kcT", [P, DEC_B, KEYS_S], F32, GI + 8960)
    vc = sb("vc", [P, DEC_B, KV_W], F32, GI + 8960 + 4352)
    prob = sb("prob", [P, 2, G, 2 * WIN], F32, Fr)
    probT = sb("probT", [P, 2, 2, G * WIN], F32, Fr + 8192)
    qs = sb("qs", [P, DEC_B, G * DEC_T], F32, Fr + 16384)
    prob_s = sb("prob_s", [P, 4, KEYS_S], F32, Fr)
    new_s = sb("new_s", [P, 4, T_S], F32, Fr + 2560)
    k_out = sb("k_out", [P, 2, KV_W], F32, Fr + 4096)
    mx = small("mx", [P, 2, 4])
    nmx = small("nmx", [P, 2, 4])
    sd = small("sd", [P, 2, 4])
    den = small("den", [P, 2, 4])
    rden = small("rden", [P, 2, 4])
    n = GI
    Gt = sb("Gt", [P, 2, MH, P], F32, n)
    DT = sb("DT", [P, MH, P], F32, n + 4096)
    SD = sb("SD", [P, MH, P], F32, n + 6144)
    kw = sb("kw", [P, MH, P], F32, n + 8192)
    hs = sb("hs", [P, MH, P], F32, n + 10240)
    Cst = sb("Cst", [P, MH, W1], F32, n + 12288)
    Cs = sb("Cs", [P, DEC_B, W1], F32, n + 14368)
    vmk = sb("vmk", [T_S, 4, W1], F32, n + 18496)
    kws = sb("kws", [T_S, MH, P], F32, n + 20576)
    SDs = sb("SDs", [T_S, MH, T_S], F32, n + 22624)
    ITs = sb("ITs", [P, MH, T_S], F32, n + 23648)
    prod = sb("prod", [P, MH, T_S], F32, n + 24672)
    hden = small("hden", [P, 4])
    hab = small("hab", [P, 4])
    hrd = small("hrd", [P, 4])
    hss = small("hss", [P, 4])
    hf = small("hf", [P, 4])
    wss = small("wss", [T_S, MH])
    n_p = small("n_p", [P, MH])
    ah = sb("ah", [P, CW], F32R, E)
    al = sb("al", [P, CW], F32R, E + 4 * CW)
    assert 8 * CW <= C - E
    wah = sb("wah", [P, 4, D], F32R, Fr)
    wal = sb("wal", [P, 4, D], F32R, Fr + 16384)
    sg_za = sb("sg_za", [P, 2, T], F32, Fr + 32768)
    sg = sb("sg", [P, 2, 364], F32, Fr + 32768 + 8 * T)
    assert Fr + 32768 + 8 * T + 8 * 364 <= end
    mh_ = sb("mh", [P, CW], F32R, A)
    ml_ = sb("ml", [P, CW], F32R, A + 4 * CW)
    wbh = sb("wbh", [P, 4, D], F32R, A + 8 * CW)
    wbl = sb("wbl", [P, 4, D], F32R, A + 8 * CW + 16384)
    x_res = sb("x_res", [P, 2, D], F32, H + 8192)
    y_out = sb("y_out", [P, 2, D], F32, H + 16384)
    g_post_b = sb("g_post_b", [P, D], F32, B)
    junk5 = sb("junk5", [P, D], F32, B + 4096)

    ps = nc.alloc_psum_tensor("ps", [P, 8, 512], F32)
    sems = {}

    def s(name):
        if name not in sems:
            sems[name] = nc.alloc_semaphore(name)
        return sems[name]

    class Step:

        def __init__(self, eng, name):
            self.eng, self.sem, self.n = eng, s(name), 0

        def __call__(self, ins):
            self.n += 1
            ins.then_inc(self.sem, 1)
            self.eng.wait_ge(self.sem, self.n)

    def wait(eng, name, value):
        if value > 0:
            eng.wait_ge(s(name), value)

    def x_cols(t):
        return P * t, P if t < NC else T_S

    def kx(part, off, width):
        return part[:, 0:KT * T].rearrange("p (k t) -> p k t", k=KT)[:, :, off:off + width]

    def bank_pair(b, n, width=512):
        return ps[0:n, b:b + 2, 0:width]

    COL_GROUPS = [(slice(0, 5), P), (slice(5, NC), P), (slice(NC, NTILE), T_S)]

    def row_cols(q, cs, n):
        c0 = 5 * (cs.start // 5)
        return ps[0:n, c0 // 5, 0:5 * NR].rearrange("p (c r) -> p c r", r=NR)[:, cs.start - c0:cs.stop - c0, q * PQ:q * PQ + MH]

    def sub_of(sub):
        j, (off, w) = sub // 3, SUBS[sub % 3]
        kind = TILES[j]
        return j, kind, j - FIRST[kind], off, w

    def unit_tokens(u):
        return (NC, T_P, T_S) if u == 0 else (u - 1, P * (u - 1), P)

    H_ORDER = list(range(1, NC + 1)) + [0]
    N_ATT = 2 * NC + 1
    N_ROUND = 2 * MH

    block = nc.Block()
    block.__enter__()

    @block.sync
    def _(sp):
        def load_x(t):
            _, n = x_cols(t)
            wait(sp, "xT_done", t - 3)
            src = i["x_prompt"][0, P * t:P * (t + 1), :] if t < NC else i["x_sample"].rearrange("b t d -> (b t) d")
            sp.dma_start(x_raw[0:n, t % 4, :], src).then_inc(s(f"x_ld{t % 4}"), 16)

        def load_wt(g):
            sp.dma_start(wt_raw[:, 2 * g:2 * g + 2, :], i["w_tok"][:, 2 * g:2 * g + 2, :]).then_inc(s(f"wt_ld{g}"), 16)

        load_x(0)
        sp.dma_start(ident[:], i["ident"]).then_inc(s("ident_ld"), 16)
        sp.dma_start(g_pre_b[:], i["g_pre"].partition_broadcast(P).rearrange("p a d -> p (a d)")).then_inc(s("gpre_ld"), 16)
        load_wt(0)
        load_x(1)
        load_wt(1)
        load_wt(2)
        load_wt(3)
        load_x(2)
        load_x(3)
        sp.dma_start(masks32[:, 0, :], i["chunk_mask"]).then_inc(s("mask_ld"), 16)
        sp.dma_start(masks32[0:T_S, 1, 0:T_S], i["seq_mask"]).then_inc(s("mask_ld"), 16)
        misc = [(gmh[:], i["g_mh_T"]), (sink_p[:], i["sinks_prompt"]), (sink_s[:], i["sinks_sample"]),
                (seqsel[:], i["seq_select"]), (newmask[:], i["new_key_mask"]), (n_s[:], i["state_n_T"]),
                (bgi[:], i["b_gate"][0:MH, :]), (bgf[PQ:PQ + MH, :], i["b_gate"][MH:2 * MH, :]), (m0T[:], i["state_m_T"])]
        for dst, src in misc:
            sp.dma_start(dst, src).then_inc(s("misc_ld"), 16)
        for t in range(4, NTILE):
            load_x(t)

        def load_w(n):
            wait(sp, "w_lo", n - 1)
            kind, j = SEQ[n]
            sp.dma_start(w_raw[:, n % 2, :], i["w_in_tiles"][j] if kind == "in" else i["w_out_tiles"][j]).then_inc(s(f"w_ld{n % 2}"), 16)

        wait(sp, "wt_split_d", 3)
        wait(sp, "wt_split_p", 1)
        load_w(0)
        load_w(1)
        wait(sp, "tok_done", NTILE)
        sp.dma_start(resets[:], i["resets"]).then_inc(s("resets_ld"), 16)
        wait(sp, "masks_done", 1)
        wait(sp, "rows_ps", 1)
        sp.dma_start(kcT[:, :, 0:WIN], i["cache_k_T"]).then_inc(s("att_ld"), 16)
        sp.dma_start(vc[:], i["cache_win_v"][0].rearrange("b w k d -> w b (k d)")).then_inc(s("att_ld"), 16)
        sp.dma_start(bias_p[:], i["bias_prompt"]).then_inc(s("att_ld"), 16)
        sp.dma_start(bias_s[:], i["bias_sample"]).then_inc(s("att_ld"), 16)
        for name, cache in (("win_k_sample", "cache_win_k"), ("win_v_sample", "cache_win_v")):
            sp.dma_start(o[name][0, :, 0:WIN - DEC_T].rearrange("b w k d -> b (w k d)"),
                         i[cache][0, :, DEC_T:WIN].rearrange("b w k d -> b (w k d)")).then_inc(s("out"), 16)
        load_w(2)
        wait(sp, "rows_done", 1)
        sp.dma_start(o["m_last_T"], m_last[:]).then_inc(s("m_out"), 16)

        def load_c(r):
            h, bs = r // 2, slice(4 * (r % 2), 4 * (r % 2) + 4)
            if r >= 2:
                sp.wait_ge(s(f"c_st{r % 2}"), 16 * h)
            sp.dma_start(Cs[:, bs, 0:MD], i["state_C"][0, bs, h].rearrange("b d v -> d b v")).then_inc(s(f"c_ld{r % 2}"), 16)

        def store_c(r):
            h, bs = r // 2, slice(4 * (r % 2), 4 * (r % 2) + 4)
            wait(sp, "round_upd", r + 1)
            sp.dma_start(o["C_sample"][0, bs, h].rearrange("b d v -> d b v"), Cs[:, bs, 0:MD]).then_inc(s(f"c_st{r % 2}"), 16)

        for n in range(3, len(SEQ)):
            kind, j = SEQ[n]
            if (kind, j) == ("in", FIRST["km"] + 2):
                sp.dma_start(o["win_v_prompt"].rearrange("a b w k d -> w (a b k d)"), va[:, NC - 1, :]).then_inc(s("v_out"), 16)
                sp.dma_start(o["win_v_sample"][0, :, WIN - DEC_T:WIN].rearrange("b t k d -> b t (k d)"),
                             va[0:T_S, NC, :]).then_inc(s("v_out"), 16)
            if (kind, j) == ("in", FIRST["za"] + 1):
                wait(sp, "ko_evac", 1)
                sp.dma_start(o["win_k_prompt"].rearrange("a b w k d -> w (a b k d)"), k_out[:, 0, :]).then_inc(s("k_outd"), 16)
                sp.dma_start(o["win_k_sample"][0, :, WIN - DEC_T:WIN].rearrange("b t k d -> b t (k d)"),
                             k_out[0:T_S, 1, :]).then_inc(s("k_outd"), 16)
                wait(sp, "pv_done", N_ATT)
                wait(sp, "scored", N_ATT)
                load_c(0)
                load_c(1)
            if (kind, j) == ("in", FIRST["za"] + 3):
                for r in range(2):
                    store_c(r)
                    load_c(r + 2)
            if (kind, j) == ("in", FIRST["om"]):
                for r in range(2, N_ROUND):
                    store_c(r)
                    if r + 2 < N_ROUND:
                        load_c(r + 2)
                sp.dma_start(o["n_sample_T"], n_s[:]).then_inc(s("out"), 16)
                wait(sp, "st_done", NC)
                sp.dma_start(o["C_prompt"].rearrange("a b h d v -> d (a b h) v"), Cst[:, :, 0:MD]).then_inc(s("cp_st"), 16)
                wait(sp, "np_done", 1)
                sp.dma_start(o["n_prompt_T"], n_p[:]).then_inc(s("cp_st"), 16)
            load_w(n)

        def load_res(t):
            _, n = x_cols(t)
            wait(sp, "y_stored", 0)
            if t >= 2:
                wait(sp, "y_ready", t - 1)
            src = i["x_prompt"][0, P * t:P * (t + 1), :] if t < NC else i["x_sample"].rearrange("b t d -> (b t) d")
            sp.dma_start(x_res[0:n, t % 2, :], src).then_inc(s(f"xr_ld{t % 2}"), 16)

        wait(sp, "ag_done", G)
        wait(sp, "ah_done", G)
        sp.dma_start(g_post_b[:], i["g_post"].partition_broadcast(P).rearrange("p a d -> p (a d)")).then_inc(s("gpost_ld"), 16)
        wait(sp, "sub_done", NSUB)
        load_res(0)
        load_res(1)
        for t in range(NTILE):
            _, n = x_cols(t)
            wait(sp, "y_ready", t + 1)
            dst = o["y_prompt"][0, P * t:P * (t + 1), :] if t < NC else o["y_sample"].rearrange("b t d -> (b t) d")
            sp.dma_start(dst, y_out[0:n, t % 2, :]).then_inc(s(f"y_st{t % 2}"), 16)
            if t + 2 < NTILE:
                load_res(t + 2)
        sp.wait_ge(s("y_st0"), 16 * 5)
        sp.wait_ge(s("y_st1"), 16 * 4)
        sp.wait_ge(s("out"), 16 * 3)
        sp.wait_ge(s("m_out"), 16)
        sp.wait_ge(s("v_out"), 32)
        sp.wait_ge(s("k_outd"), 32)
        sp.wait_ge(s("c_st0"), 16 * MH)
        sp.wait_ge(s("c_st1"), 16 * MH)
        sp.wait_ge(s("cp_st"), 32)

    @block.tensor
    def _(pe):
        mm = nc.tensor.matmul
        state = {"sub": 0, "at": 0}

        def x_transpose(t):
            off, n = x_cols(t)
            b = 2 * (t % 2)
            wait(pe, "xn_ready", t + 1)
            wait(pe, "x_split", t - 1)
            if t == 0:
                pe.wait_ge(s("ident_ld"), 16)
            for kk in range(KT):
                last = nc.tensor.transpose(ps[:, b + kk // 4, (kk % 4) * P:(kk % 4) * P + n],
                                           x_raw[0:n, t % 4, kk * P:(kk + 1) * P], ident[0:n, 0:n])
            last.then_inc(s("xT_done"), 1)

        def token_major(t, ks):
            off, _ = x_cols(t)
            b = 4 + 2 * (t % 2)
            wait(pe, "x_split", t + 1)
            wait(pe, "tok_act", t - 1)
            wait(pe, "tok_dve", t - 1)
            if t == 0:
                wait(pe, "pads", 1)
            for kk in ks:
                if t == 0 and kk % 2 == 0:
                    wait(pe, "wt_split_d", [1, 2, 2, 3][kk // 2])
                    wait(pe, "wt_split_p", [0, 0, 1, 1][kk // 2])
                lhs_h = xh[:, kk * T + off:kk * T + off + P]
                lhs_l = xl[:, kk * T + off:kk * T + off + P]
                for q in range(2):
                    cols = slice(q * TOK_H, (q + 1) * TOK_H)
                    out = ps[:, b + q, 0:TOK_H]
                    mm(out, lhs_h, wt_hi[:, kk, cols], start=(kk == 0), stop=False)
                    mm(out, lhs_h, wt_lo[:, kk, cols], start=False, stop=False)
                    last = mm(out, lhs_l, wt_hi[:, kk, cols], start=False, stop=(kk == KT - 1))
            if ks[-1] == KT - 1:
                last.then_inc(s("tok_done"), 1)

        def project(n):
            for _ in range(n):
                sub, at_ = state["sub"], state["at"]
                j, kind, _, off, w = sub_of(sub)
                if at_ == 0:
                    if sub < 2:
                        wait(pe, "tok_act", NC)
                        wait(pe, "tok_dve", NC)
                    else:
                        wait(pe, "proj_free", sub - 1)
                    if sub % 3 == 0:
                        wait(pe, "w_lo", POS[("in", j)] + 1)
                kk, pas = at_ // 3, at_ % 3
                wt = (w_lo if pas == 2 else w_hi)[:, j % 2, kk * P:(kk + 1) * P]
                xt = (xl if pas == 1 else xh)[:, kk * T + off:kk * T + off + w]
                last = mm(ps[:, 6 + sub % 2, 0:w], wt, xt, start=(at_ == 0), stop=(at_ == 23))
                state["at"] += 1
                if state["at"] == 24:
                    last.then_inc(s("sub_done"), 1)
                    state["sub"], state["at"] = sub + 1, 0

        x_transpose(0)
        token_major(0, range(0, 4))
        x_transpose(1)
        token_major(0, range(4, KT))
        for t in range(1, NTILE):
            if t + 1 < NTILE:
                x_transpose(t + 1)
            token_major(t, range(KT))

        project(24)
        wait(pe, "tok_dve", NTILE)
        wait(pe, "tok_act", NTILE)
        wait(pe, "x_split", NTILE)
        for c in range(NTILE):
            _, n = x_cols(c)
            last = nc.tensor.transpose(ps[0:PQ + MH, c // 4, (c % 4) * P:(c % 4) * P + n], gates[0:n, c, 0:PQ + MH], ident[0:n, 0:n])
        last.then_inc(s("rows_ps"), 1)
        project(24 * 8)
        wait(pe, "rows_done", 1)
        for c in range(NTILE):
            off, n = x_cols(c)
            nc.tensor.transpose(ps[0:n, c // 5, (c % 5) * NR:(c % 5 + 1) * NR], rows[:, off:off + n], ident[0:NR, 0:NR])
        mm(ps[:, 2, 0:NC * MH], ones[0:MH, 0:1].broadcast_to([MH, P]), mpd[:].rearrange("k c h -> k (c h)"), start=True, stop=True)\
            .then_inc(s("cols_ps"), 1)
        project(24 * S_P2 - 24 * 9)

        def scores(u):
            wait(pe, "scored", u)
            if u == 0:
                wait(pe, "proj_free", S_P2 - 2)
                wait(pe, "cols_done", 1)
            if u < 2 * NC:
                blk, kv = u // 2, u % 2
                rows = slice(kv * HD, (kv + 1) * HD)
                k0 = 1 if blk == 0 else 0
                for g in range(G):
                    last = mm(ps[:, g // 2, (g % 2) * 256 + k0 * WIN:(g % 2) * 256 + 256],
                              qaT[rows, g, blk * P:(blk + 1) * P],
                              kaT[rows, (blk - 1 + k0) * P:(blk + 1) * P], start=True, stop=True)
            else:
                wait(pe, "qs_ready", 1)
                for kv in range(KVH):
                    rows = slice(kv * HD, (kv + 1) * HD)
                    for b in range(DEC_B):
                        r = 32 * (b % 4)
                        last = mm(ps[r:r + 32, kv, (b // 4) * KEYS_S:(b // 4 + 1) * KEYS_S], qs[rows, b, :], kcT[rows, b, :],
                                  start=True, stop=True)
            last.then_inc(s("qk_done"), 1)

        def prob_transposes(u):
            wait(pe, "prob_ready", u + 1)
            wait(pe, "pT_act", u)
            wait(pe, "pT_dve", u - 2)
            if u < 2 * NC:
                for kb in range(1 if u < 2 else 0, 2):
                    for g in range(G):
                        last = nc.tensor.transpose(ps[:, 2 + kb, g * P:(g + 1) * P],
                                                   prob[:, u % 2, g, kb * WIN:(kb + 1) * WIN], ident[:])
            else:
                for q in range(4):
                    nc.tensor.transpose(ps[:, 2, q * P:(q + 1) * P], prob_s[:, q, 0:WIN], ident[:])
                for q in range(4):
                    last = nc.tensor.transpose(ps[0:T_S, 3, q * P:(q + 1) * P], new_s[:, q, :], ident[:])
            last.then_inc(s("pTr_done"), 1)

        def values(u):
            wait(pe, "pT_act", u + 1)
            wait(pe, "pT_dve", u - 1)
            wait(pe, "att_out", u - 1)
            if u < 2 * NC:
                blk, kv = u // 2, u % 2
                out = ps[kv * HD:(kv + 1) * HD, 4 + u % 2, :]
                for kb in range(1 if blk == 0 else 0, 2):
                    last = mm(out, va[:, blk - 1 + kb, kv * HD:(kv + 1) * HD], probT[:, u % 2, kb, :],
                              start=(kb == 1 or blk > 0) and (kb == 0 or blk == 0), stop=(kb == 1))
            else:
                for kv in range(KVH):
                    rows = slice(kv * HD, (kv + 1) * HD)
                    mm(ps[rows, 4, 0:2 * P], va[0:T_S, NC, rows], probT[0:T_S, 0, 1, kv * 2 * P:(kv + 1) * 2 * P],
                       start=True, stop=False, skip_group_check=True)
                    for b in range(DEC_B):
                        last = mm(ps[rows, 4, b * 32:(b + 1) * 32], vc[:, b, rows],
                                  probT[:, 0, 0, kv * 2 * P + b * 32:kv * 2 * P + (b + 1) * 32],
                                  start=False, stop=(b == DEC_B - 1), skip_group_check=True)
            last.then_inc(s("pv_done"), 1)

        for it in range(S_P3 - S_P2):
            if it < N_ATT:
                scores(it)
            project(24)
            if 1 <= it <= N_ATT:
                prob_transposes(it - 1)
            if 2 <= it <= N_ATT + 1:
                values(it - 2)
            if it == N_ATT + 1:
                nc.tensor.transpose(ps[:, 0, 0:P], kaT[:, T_P - P:T_P], ident[:])
                nc.tensor.transpose(ps[0:T_S, 0, P:2 * P], kaT[:, T_P:T], ident[:]).then_inc(s("ko_ps"), 1)

        def log_weights(u):
            c, off, n = unit_tokens(u)
            wait(pe, "kw_done", u)
            if u == 0:
                wait(pe, "ko_evac", 1)
                for h in range(MH):
                    mm(ps[:, 0, 256 + h * n:256 + (h + 1) * n], glc[:, h:h + 1].broadcast_to([n, P]), ident[0:n, 0:n],
                       start=(h == 0), stop=False, skip_group_check=True)
            for h in range(MH):
                last = mm(ps[0:n, 0, h * n:(h + 1) * n], r1c[0:n, c, h:h + 1].broadcast_to([n, n]), ident[0:n, 0:n],
                          start=(h == 0 and u > 0), stop=False, skip_group_check=True)
            last.then_inc(s("r1_done"), 1)

        def log_mask(u):
            _, _, n = unit_tokens(u)
            wait(pe, "g_done", u + 1)
            m = (mask_b if u else seqmask_b)[0:n, 0:n].unsqueeze(1).broadcast_to([n, MH, n])
            mm(ps[0:n, 0, 0:MH * n], ident_b[0:n, 0:n], m, start=False, stop=True, skip_group_check=True)\
                .then_inc(s("mask_done"), 1)

        def m_scores(u):
            _, off, n = unit_tokens(u)
            wait(pe, "sd_done", u)
            wait(pe, "hT_evac", u - 2)
            if u == 0:
                wait(pe, "proj_free", S_P3)
            for h in range(MH):
                last = mm(ps[0:n, 1, h * n:(h + 1) * n], kmT[:, h, off:off + n], qmT[:, h, off:off + n], start=True, stop=True)
            last.then_inc(s("s_done"), 1)

        def k_transposes(u):
            _, off, n = unit_tokens(u)
            wait(pe, "d_done", u + 1)
            for h in range(MH):
                last = nc.tensor.transpose(ps[0:n, 0, h * P:(h + 1) * P], kmT[:, h, off:off + n], ident[:])
            last.then_inc(s("kT_done"), 1)

        def numerator(u):
            c, off, n = unit_tokens(u)
            v = H_ORDER.index(u) + 1
            wait(pe, "sd_done", u + 1)
            wait(pe, "qg_done", u + 1)
            wait(pe, "h_done", v - 1)
            if u == 0:
                wait(pe, "it_evac", N_ROUND)
                wait(pe, "prod_done", MH)
            else:
                wait(pe, "st_done", u - 1)
            for h in range(MH):
                out = ps[0:n, 2 + h // 2, (h % 2) * W1:(h % 2 + 1) * W1]
                last = mm(out, (SD if u else SDs)[0:n, h, :], vm1[0:n, c, h, :], start=True, stop=(u == 1), skip_group_check=True)
                if u > 1:
                    last = mm(out, qmT[:, h, off:off + n], Cst[:, h, :], start=False, stop=True, skip_group_check=True)
                if u == 0:
                    mm(out[:, 0:MD], ITs[:, h, :], ident[:], start=False, stop=False, skip_group_check=True)
                    last = mm(out[:, MD:W1], prod[:, h, :], ones[:], start=False, stop=True, skip_group_check=True)
            last.then_inc(s("num_done"), 1)

        def state_update(u):
            c, _, _ = unit_tokens(u)
            wait(pe, "kw_done", u + 1)
            wait(pe, "round_upd", min(u, N_ROUND))
            for h in range(MH):
                last = mm(ps[:, 4 + h // 2, (h % 2) * W1:(h % 2 + 1) * W1], kw[:, h, :], vm1[:, c, h, :], start=True, stop=True)
            last.then_inc(s("cup_done"), 1)

        def sample_inter(r):
            h, hf_ = r // 2, r % 2
            wait(pe, "st_done", r)
            pe.wait_ge(s(f"c_ld{hf_}"), 16 * (h + 1))
            wait(pe, "qg_done", 1)
            for b in range(4 * hf_, 4 * hf_ + 4):
                last = mm(ps[:, 4, 320 + 8 * b:328 + 8 * b], Cs[:, b, 0:MD],
                          qmT[:, h, T_P + DEC_T * b:T_P + DEC_T * (b + 1)], start=True, stop=True)
            last.then_inc(s("it_done"), 1)

        def sample_round(r):
            h, hf_ = r // 2, r % 2
            wait(pe, "st_done", r)
            wait(pe, "it_evac", r + 1)
            wait(pe, "kw_done", 1)
            wait(pe, "vmk_done", r + 1)
            for q in range(2):
                last = mm(ps[:, 4 + q, 0:2 * W1], kws[:, h, :], vmk[:, 2 * q:2 * q + 2, :].rearrange("p b v -> p (b v)"),
                          start=True, stop=True)
            last.then_inc(s("rcup_done"), 1)

        def h_transposes(u, it):
            _, _, n = unit_tokens(u)
            v = H_ORDER.index(u) + 1
            wait(pe, "h_done", v)
            wait(pe, "sd_done", min(it + 1, NTILE))
            wait(pe, "hT_evac", v - 1)
            for h in range(MH):
                last = nc.tensor.transpose(ps[:, 1, h * n:(h + 1) * n], hs[0:n, h, :], ident[0:n, 0:n])
            last.then_inc(s("hT_done"), 1)

        for it in range(S_P4 - S_P3):
            if it <= NC:
                log_weights(it)
            if 2 <= it <= NC + 1:
                numerator(it - 1)
                state_update(it - 1)
            project(7)
            if it == NC + 2:
                h_transposes(NC, it)
                numerator(0)
            if it == NC + 3:
                h_transposes(0, it)
            if it <= NC:
                m_scores(it)
            if 1 <= it <= N_ROUND:
                sample_inter(it - 1)
            if it <= NC:
                log_mask(it)
            project(7)
            if 1 <= it <= N_ROUND:
                sample_round(it - 1)
            if it <= NC:
                k_transposes(it)
            if 2 <= it <= NC:
                h_transposes(it - 1, it)
            project(10)

        project(24 * (NSUB - S_P4))

        def out_part(t, ks):
            off, _ = x_cols(t)
            b = 2 * (t % 4)
            for kk in ks:
                if t == 0:
                    if kk < 4:
                        wait(pe, "al_done", kk + 1)
                        wait(pe, "w_lo", POS[("out", kk)] + 1)
                    else:
                        wait(pe, "ml_done", kk - 3)
                        wait(pe, "w_lo", POS[("out", kk)] + 1)
                hi, lo, wh, wl = (ah, al, wah, wal) if kk < 4 else (mh_, ml_, wbh, wbl)
                c0 = (kk % 4) * T + off
                for q in range(2):
                    cols = slice(512 * q, 512 * (q + 1))
                    out = ps[:, b + q, :]
                    mm(out, hi[:, c0:c0 + P], wh[:, kk % 4, cols], start=(kk == 0), stop=False, skip_group_check=True)
                    mm(out, hi[:, c0:c0 + P], wl[:, kk % 4, cols], start=False, stop=False, skip_group_check=True)
                    last = mm(out, lo[:, c0:c0 + P], wh[:, kk % 4, cols], start=False, stop=(kk == KT - 1), skip_group_check=True)
            if ks[-1] == KT - 1:
                last.then_inc(s("y_done"), 1)

        wait(pe, "hT_evac", NTILE)
        wait(pe, "h_done", NTILE)
        for t in range(4):
            if t == 3:
                wait(pe, "proj_free", NSUB)
            out_part(t, list(range(4)))
        for t in range(4):
            out_part(t, list(range(4, KT)))
        for t in range(4, NTILE):
            wait(pe, "y_free", t - 3)
            if t == NTILE - 1:
                wait(pe, "pads", 2)
            out_part(t, list(range(KT)))

    @block.scalar
    def _(act):
        A_ = nc.scalar.activation
        step = Step(act, "act_step")

        def square(t):
            _, n = x_cols(t)
            act.wait_ge(s(f"x_ld{t % 4}"), 16 * (t // 4 + 1))
            wait(act, "ss_ready", t)
            A_(junk[0:n, :], x_raw[0:n, t % 4, :], ACT.Square, accum_out=stat[0:n, t:t + 1]).then_inc(s("ss_ready"), 1)

        def x_hi(t):
            off, n = x_cols(t)
            b = 2 * (t % 2)
            wait(act, "xT_done", t + 1)
            A_(kx(xh, off, n), bank_pair(b, P).rearrange("p b (k t) -> p (b k) t", k=4)[:, :, 0:n], ACT.Copy).then_inc(s("xh_ready"), 1)

        def token_evac(t):
            _, n = x_cols(t)
            b = 4 + 2 * (t % 2)
            wait(act, "tok_done", t + 1)
            A_(vm1[0:n, t, :, 0:MD].rearrange("p (b h) v -> p b h v", b=2),
               bank_pair(b, n, 2 * MD).rearrange("p b (h v) -> p b h v", h=2), ACT.Copy)
            A_(va[0:n, t, 0:VA0], ps[0:n, b, 2 * MD:TOK_H], ACT.Copy).then_inc(s("tok_act"), 1)

        def split_hi(n):
            kind, j = SEQ[n]
            if kind == "in":
                wait(act, "sub_done", 3 * (j - 1))
                dst = w_hi[:, j % 2, :]
            elif j < 4:
                if j == 0:
                    wait(act, "ag_done", G)
                    act.wait_ge(s("cp_st"), 32)
                    act.wait_ge(s("c_st0"), 16 * MH)
                    act.wait_ge(s("c_st1"), 16 * MH)
                dst = wah[:, j, :]
            else:
                wait(act, "sub_done", NSUB)
                dst = wbh[:, j - 4, :]
            act.wait_ge(s(f"w_ld{n % 2}"), 16 * (n // 2 + 1))
            A_(dst, w_raw[:, n % 2, :], ACT.Copy).then_inc(s("w_hi"), 1)

        def evac(sub):
            j, kind, t, off, w = sub_of(sub)
            cols = slice(off, off + w)
            wait(act, "sub_done", sub + 1)
            src = ps[:, 6 + sub % 2, 0:w]
            if kind in ("om", "zm"):
                m = sub - S_P4
                wait(act, "sg_used", m - 1)
                if m == 0:
                    wait(act, "hT_evac", NTILE)
                A_(sg[:, m % 2, 0:w], src, ACT.Sigmoid).then_inc(s("proj_free" if kind == "om" else "sgz_ready"), 1)
            else:
                if sub == 3 * FIRST["km"]:
                    act.wait_ge(s("m_out"), 16)
                    wait(act, "cols_ps", 1)
                if sub == S_P3:
                    act.wait_ge(s("k_outd"), 32)
                    wait(act, "pv_done", N_ATT)
                dst = {"ka": kaT[:, cols], "qa": qaT[:, t, cols], "km": kmT[:, t, cols], "qm": qmT[:, t, cols],
                       "za": zaT[:, t, cols]}[kind]
                A_(dst, src, ACT.Copy, scale=float(MD) ** -0.5 if kind == "km" else 1.0).then_inc(s("proj_free"), 1)
            for n in PLAN.get(sub, []):
                split_hi(n)

        def wt_hi_part(g):
            act.wait_ge(s(f"wt_ld{g}"), 16)
            r = slice(2 * g, 2 * g + 2)
            A_(wt_hi[:, r, :], wt_raw[:, r, :], ACT.Copy).then_inc(s("wt_hi_a"), 1)

        square(0)
        wt_hi_part(0)
        square(1)
        for t in range(NTILE):
            x_hi(t)
            if t == 0:
                wt_hi_part(2)
            if t + 2 < NTILE:
                square(t + 2)
            if t >= 2:
                token_evac(t - 2)
        token_evac(NTILE - 2)
        wait(act, "wt_split_d", 3)
        wait(act, "wt_split_p", 1)
        split_hi(0)
        token_evac(NTILE - 1)

        for sub in range(S_P2):
            evac(sub)
            if sub == 1:
                wait(act, "abs_f", 1)
                A_(rb[:], ra[:], ACT.Exp, scale=-1.0).then_inc(s("exp_f"), 1)
            if sub == 2:
                wait(act, "one_exp", 1)
                A_(rc[:], ra[:], ACT.Ln).then_inc(s("ln_f"), 1)
            if sub == 9:
                wait(act, "cols_dve", 1)
                for cs, n in COL_GROUPS:
                    last = A_(enm[0:n, cs, :], row_cols(2, cs, n), ACT.Exp, scale=-1.0)
                last.then_inc(s("cols_done"), 1)

        def exps(u):
            wait(act, "scored", u + 1)
            b = u % 2
            k0 = WIN if u < 2 else 0
            for g in range(4):
                p = prob[:, b, g, k0:] if u < 2 * NC else prob_s[:, g, :]
                A_(p, p, ACT.Exp, bias=nmx[:, b, g:g + 1], accum_out=den[:, b, g:g + 1])
            A_(sd[:, b, :], sd[:, b, :], ACT.Exp).then_inc(s("exp_done"), 1)

        def probT_evac(u):
            wait(act, "pTr_done", u + 1)
            wait(act, "pv_done", u - 1)
            n = P if u < 2 * NC else T_S
            A_(probT[0:n, u % 2, 1, :], ps[0:n, 3, :], ACT.Copy).then_inc(s("pT_act"), 1)

        def out_evac(u):
            wait(act, "pv_done", u + 1)
            if u < 2 * NC:
                blk, kv = u // 2, u % 2
                rows = slice(kv * HD, (kv + 1) * HD)
                A_(qaT[rows, :, blk * P:(blk + 1) * P], ps[rows, 4 + u % 2, :].rearrange("p (g t) -> p g t", g=G), ACT.Copy)\
                    .then_inc(s("att_out"), 1)
            else:
                A_(qaT[:, :, T_P:T].rearrange("p g (b t) -> p b g t", t=DEC_T),
                   ps[:, 4, 0:2 * P].rearrange("p (b g t) -> p b g t", g=G, t=DEC_T), ACT.Copy).then_inc(s("att_out"), 1)

        for it in range(S_P3 - S_P2):
            if 2 <= it <= N_ATT + 1:
                probT_evac(it - 2)
            if 3 <= it <= N_ATT + 2:
                out_evac(it - 3)
            if it < N_ATT:
                exps(it)
            if it == N_ATT + 2:
                wait(act, "ko_ps", 1)
                A_(k_out[:, 0, :], ps[:, 0, 0:P], ACT.Copy)
                A_(k_out[0:T_S, 1, :], ps[0:T_S, 0, P:2 * P], ACT.Copy).then_inc(s("ko_evac"), 1)
            evac(S_P2 + it)

        def g_exp(u):
            c, _, n = unit_tokens(u)
            wait(act, "r1_done", u + 1)
            wait(act, "st_done", u - 2)
            if u == 0:
                act.wait_ge(s("v_out"), 32)
                act.wait_ge(s("att_ld"), 64)
                A_(Gt[:, 0, 0:2, :].rearrange("p h t -> p (h t)"), ps[:, 0, 256:512], ACT.Exp).then_inc(s("g_done"), 1)
            else:
                if u == 2:
                    wait(act, "qg_done", 1)
                    wait(act, "dec_done", 1)
                for h in range(MH):
                    last = A_(Gt[:, u % 2, h, :], ps[:, 0, h * P:(h + 1) * P], ACT.Exp, bias=mpb[:, c, h:h + 1])
                last.then_inc(s("g_done"), 1)

        def d_exp(u):
            c, _, n = unit_tokens(u)
            wait(act, "mask_done", u + 1)
            wait(act, "sd_done", u)
            for h in range(MH):
                last = A_(DT[0:n, h, 0:n], ps[0:n, 0, h * n:(h + 1) * n], ACT.Exp, bias=r2c[0:n, c, h:h + 1])
            last.then_inc(s("d_done"), 1)

        def k_weight(u):
            _, _, n = unit_tokens(u)
            wait(act, "kT_done", u + 1)
            act.wait_ge(s("d_done"), u + 1)
            if u == 0:
                wait(act, "wss_done", 1)
            else:
                wait(act, "cup_done", u - 1)
            for h in range(MH):
                w = DT[:, h, P - 1:P] if u else wss[:, h:h + 1]
                last = A_((kw if u else kws)[0:n, h, :], ps[0:n, 0, h * P:(h + 1) * P], ACT.Copy, scale=w)
            last.then_inc(s("kw_done"), 1)

        def h_squares(u):
            _, _, n = unit_tokens(u)
            v = H_ORDER.index(u) + 1
            wait(act, "hden_done", v)
            wait(act, "hT_done", v - 1)
            wait(act, "hq_ready", v - 1)
            for h in range(MH):
                last = A_(hs[0:n, h, :], ps[0:n, 2 + h // 2, (h % 2) * W1:(h % 2) * W1 + MD], ACT.Square,
                          accum_out=hss[0:n, h:h + 1])
            last.then_inc(s("sq_done"), 1)

        for it in range(S_P4 - S_P3):
            if it <= NC:
                g_exp(it)
            if 2 <= it <= NC + 2:
                h_squares(it - 1 if it <= NC + 1 else 0)
            if 1 <= it <= N_ROUND:
                h, c0 = (it - 1) // 2, 32 * ((it - 1) % 2)
                wait(act, "it_done", it)
                A_(ITs[:, h, c0:c0 + 32], ps[:, 4, 320 + c0:352 + c0], ACT.Copy).then_inc(s("it_evac"), 1)
            if it <= NC:
                d_exp(it)
            if it <= NC:
                k_weight(it)
            evac(S_P3 + it)

        def gate_a_sigmoid(t):
            if t == 0:
                wait(act, "hT_evac", NTILE)
                act.wait_ge(s("cp_st"), 32)
                act.wait_ge(s("c_st0"), 16 * MH)
                act.wait_ge(s("c_st1"), 16 * MH)
                wait(act, "proj_free", S_P4)
            wait(act, "za_used", t - 1)
            A_(sg_za[:, t % 2, :], zaT[:, t, :], ACT.Sigmoid).then_inc(s("sgza_ready"), 1)

        def a_hi(t):
            wait(act, "ag_done", t + 1)
            A_(ah[:, t * T:(t + 1) * T], qaT[:, t, :], ACT.Copy).then_inc(s("ah_done"), 1)

        for sub in range(S_P4, NSUB):
            m = sub - S_P4
            if m % 2 == 0 and m < 2 * G:
                gate_a_sigmoid(m // 2)
            if m % 2 == 1 and 3 <= m < 2 * G + 3:
                a_hi((m - 3) // 2)
            evac(sub)

        for j in range(MH):
            wait(act, "sg_used", 12 + 3 * (j + 1))
            wait(act, "sub_done", NSUB)
            A_(mh_[:, j * T:(j + 1) * T], qmT[:, j, :], ACT.Copy).then_inc(s("mh_done"), 1)
            split_hi(POS[("out", 4 + j)])
        for t in range(NTILE):
            _, n = x_cols(t)
            wait(act, "y_done", t + 1)
            wait(act, "ss_y", t)
            if t == 0:
                wait(act, "al_done", G)
            A_(junk5[0:n, :], bank_pair(2 * (t % 4), n).rearrange("p b c -> p (b c)"), ACT.Square,
               accum_out=stat[0:n, t:t + 1]).then_inc(s("ss_y"), 1)

    @block.vector
    def _(dve):
        V = nc.vector
        step = Step(dve, "dve_step")
        TT, TS, STT, CP = V.tensor_tensor, V.tensor_scalar, V.scalar_tensor_tensor, V.tensor_copy

        def x_norm(t):
            _, n = x_cols(t)
            wait(dve, "rstd_ready", t + 1)
            if t == 0:
                dve.wait_ge(s("gpre_ld"), 16)
            STT(out=x_raw[0:n, t % 4, :], in0=x_raw[0:n, t % 4, :], scalar=stat[0:n, NTILE + t:NTILE + t + 1],
                in1=g_pre_b[0:n, :], op0=ALU.mult, op1=ALU.mult).then_inc(s("xn_ready"), 1)

        def x_lo(t):
            off, n = x_cols(t)
            b = 2 * (t % 2)
            wait(dve, "xh_ready", t + 1)
            TT(kx(xl, off, n), bank_pair(b, P).rearrange("p b (k t) -> p (b k) t", k=4)[:, :, 0:n],
               kx(xh, off, n).bitcast(F32), ALU.subtract).then_inc(s("x_split"), 1)

        def wt_hi_part(g):
            dve.wait_ge(s(f"wt_ld{g}"), 16)
            r = slice(2 * g, 2 * g + 2)
            CP(wt_hi[:, r, :], wt_raw[:, r, :]).then_inc(s("wt_hi_d"), 1)

        def wt_lo_part(g):
            if g == 0:
                wait(dve, "wt_hi_a", 1)
            else:
                wait(dve, "wt_hi_d", 1 if g == 1 else 2)
            r = slice(2 * g, 2 * g + 2)
            TT(wt_lo[:, r, :], wt_raw[:, r, :], wt_hi[:, r, :].bitcast(F32), ALU.subtract).then_inc(s("wt_split_d"), 1)

        def token_evac(t):
            _, n = x_cols(t)
            b = 4 + 2 * (t % 2)
            wait(dve, "tok_act", t + 1)
            CP(va[0:n, t, VA0:KV_W], ps[0:n, b + 1, 2 * MD:2 * MD + KV_W - VA0])
            if t == 0:
                wait(dve, "gates_zero", 1)
            CP(gates[0:n, t, :].rearrange("p (q h) -> p q h", q=2)[:, :, 0:MH],
               ps[0:n, b + 1, TOK_H - 2 * MH:TOK_H].rearrange("p (q h) -> p q h", q=2)).then_inc(s("tok_dve"), 1)

        x_norm(0)
        wt_lo_part(0)
        x_lo(0)
        wt_hi_part(1)
        wt_lo_part(1)
        x_norm(1)
        wt_hi_part(3)
        wt_lo_part(3)
        x_lo(1)
        x_norm(2)
        dve.wait_ge(s("mask_ld"), 32)
        CP(mask_b[:], masks32[:, 0, :])
        CP(seqmask_b[:], masks32[0:T_S, 1, 0:T_S])
        dve.wait_ge(s("ident_ld"), 16)
        CP(ident_b[:], ident[:]).then_inc(s("masks_done"), 1)
        token_evac(0)
        for t in range(2, NTILE):
            if t + 1 < NTILE:
                x_norm(t + 1)
            x_lo(t)
            token_evac(t - 1)
        token_evac(NTILE - 1)

        dve.wait_ge(s("misc_ld"), 16 * 9)
        dve.wait_ge(s("resets_ld"), 16)
        wait(dve, "rows_ps", 1)
        for dst, bias, q in ((ib, bgi, 0), (fb, bgf, PQ)):
            last = TS(dst[:], ps[q:q + MH, 0:3, :].rearrange("p b t -> p (b t)")[:, 0:T], bias[q:q + MH, 0:1], None, ALU.add)
        step(last)
        STT(out=ra[:], in0=fb[:], scalar=-1.0, in1=fb[:], op0=ALU.mult, op1=ALU.max).then_inc(s("abs_f"), 1)
        wait(dve, "exp_f", 1)
        wait(dve, "rows_zero", 1)
        step(TS(ra[:], rb[:], 1.0, None, ALU.add))
        STT(out=re_, in0=ra[:], scalar=1.0, in1=rb[:], op0=ALU.subtract, op1=ALU.subtract).then_inc(s("one_exp"), 1)
        wait(dve, "ln_f", 1)
        step(STT(out=rc[:], in0=fb[:], scalar=0.0, in1=rc[:], op0=ALU.min, op1=ALU.subtract))
        step(TT(rc[:], rc[:], re_, ALU.add))
        V.tensor_tensor_scan(out=ra[:], data0=resets[:], data1=rc[:], initial=0.0, op0=ALU.mult, op1=ALU.add)
        V.tensor_tensor_scan(out=rd[:, 0:T_P], data0=rc[:, 0:T_P], data1=ib[:, 0:T_P], initial=0.0, op0=ALU.add, op1=ALU.max)
        for b in range(DEC_B):
            c0 = T_P + DEC_T * b
            last = V.tensor_tensor_scan(out=rd[:, c0:c0 + DEC_T], data0=rc[:, c0:c0 + DEC_T], data1=ib[:, c0:c0 + DEC_T],
                                        initial=m0T[:, b:b + 1], op0=ALU.add, op1=ALU.max)
        step(last)
        CP(m_last[:, 0:1], rd[:, T_P - 1:T_P])
        CP(m_last[:, 1:1 + DEC_B], rd[:, T_P:T].rearrange("h (b t) -> h b t", t=DEC_T)[:, :, DEC_T - 1])
        V.memset(mp[:, 0:1], 0.0)
        CP(mp[:, 1:NC], rd[:, P - 1:T_P - P:P])
        step(CP(mp[:, NC:NC + DEC_B], m0T[:]))
        step(TT(re_, ra[:], rd[:], ALU.subtract))
        TT(rf, ib[:], ra[:], ALU.subtract)
        CP(r_m, rd[:])
        TT(r_gl[:, T_P:T].rearrange("h (b t) -> h b t", t=DEC_T), re_[:, T_P:T].rearrange("h (b t) -> h b t", t=DEC_T),
           mp[:, NC:NC + DEC_B].unsqueeze(2).broadcast_to([MH, DEC_B, DEC_T]), ALU.add)
        TT(mpd[:], mp[:, 0:NC].unsqueeze(2).broadcast_to([MH, NC, MH]),
           ident[0:MH, 0:MH].unsqueeze(1).broadcast_to([MH, NC, MH]), ALU.mult).then_inc(s("rows_done"), 1)
        wait(dve, "cols_ps", 1)
        for q, dst in enumerate((r1c, r2c)):
            for cs, n in COL_GROUPS:
                CP(dst[0:n, cs, :], row_cols(q, cs, n))
        CP(glc[:], row_cols(3, slice(NC, NTILE), T_S).rearrange("p c h -> p (c h)"))
        CP(mpb[:], ps[:, 2, 0:NC * MH].rearrange("p (c h) -> p c h", h=MH)).then_inc(s("cols_dve"), 1)

        def score(u):
            wait(dve, "qk_done", u + 1)
            wait(dve, "pTr_done", u - 1)
            b = u % 2
            if u == 0:
                dve.wait_ge(s("att_ld"), 64)
            if u < 2 * NC:
                kv = u % 2
                k0 = WIN if u < 2 else 0
                p = prob[:, b, :, k0:]
                step(STT(out=p, in0=ps[:, 0:2, :].rearrange("p b (g k) -> p (b g) k", g=2)[:, :, k0:], scalar=float(HD) ** -0.5,
                         in1=bias_p[:, kv * G:(kv + 1) * G, k0:], op0=ALU.mult, op1=ALU.add))
                sink = sink_p[:, kv * G:(kv + 1) * G]
            else:
                for kv in range(KVH):
                    last = STT(out=prob_s[:, 2 * kv:2 * kv + 2, :], in0=ps[:, kv, 0:2 * KEYS_S].rearrange("p (a k) -> p a k", a=2),
                               scalar=float(HD) ** -0.5, in1=bias_s[:, kv:kv + 1, :].broadcast_to([P, 2, KEYS_S]),
                               op0=ALU.mult, op1=ALU.add)
                step(last)
                p, sink = prob_s[:], sink_s[:]
            step(V.tensor_reduce(mx[:, b, :], p, AX_X, ALU.max))
            step(TT(mx[:, b, :], mx[:, b, :], sink, ALU.max))
            TS(nmx[:, b, :], mx[:, b, :], -1.0, None, ALU.mult)
            TT(sd[:, b, :], sink, mx[:, b, :], ALU.subtract).then_inc(s("scored"), 1)

        def denominators(u):
            b = u % 2
            wait(dve, "exp_done", u + 1)
            step(TT(den[:, b, :], den[:, b, :], sd[:, b, :], ALU.add))
            V.reciprocal(rden[:, b, :], den[:, b, :]).then_inc(s("rden_done"), 1)

        def probT_evac(u):
            wait(dve, "pTr_done", u + 1)
            wait(dve, "pv_done", u - 1)
            CP(probT[:, u % 2, 0, :], ps[:, 2, :]).then_inc(s("pT_dve"), 1)

        for it in range(S_P3 - S_P2):
            if 1 <= it <= N_ATT:
                denominators(it - 1)
            if 4 <= it <= N_ATT + 1:
                probT_evac(it - 2)
            if it == 2:
                CP(qs[:].rearrange("p b (g t) -> p b g t", g=G), qaT[:, :, T_P:T].rearrange("p g (b t) -> p b g t", t=DEC_T))
                CP(kcT[:, :, WIN:KEYS_S], kaT[:, T_P:T].rearrange("p (b t) -> p b t", t=DEC_T)).then_inc(s("qs_ready"), 1)
            if it < N_ATT:
                score(it)

        def sd_mul(u):
            _, _, n = unit_tokens(u)
            wait(dve, "d_done", u + 1)
            wait(dve, "s_done", u + 1)
            wait(dve, "num_done", u - 1)
            TT((SD if u else SDs)[0:n, :, :], ps[0:n, 1, 0:MH * n].rearrange("p (h t) -> p h t", h=MH), DT[0:n, :, 0:n], ALU.mult)\
                .then_inc(s("sd_done"), 1)

        def q_gate(u):
            _, off, n = unit_tokens(u)
            wait(dve, "g_done", u + 1)
            wait(dve, "s_done", u + 1)
            g = Gt[:, u % 2, :, :] if u else Gt[:, 0, 0:2, :].rearrange("p a (h t) -> p (a h) t", t=T_S)
            q = qmT[:, :, off:off + n]
            TT(q, q, g, ALU.mult).then_inc(s("qg_done"), 1)

        def sample_extras():
            g = Gt[:, 0, 0:2, :].rearrange("p a (h b t) -> p (a h) b t", b=DEC_B, t=DEC_T)
            CP(dec_s[:].rearrange("p b h -> p h b"), g[:, :, :, DEC_T - 1]).then_inc(s("dec_done"), 1)
            V.tensor_reduce(wss[:], DT[0:T_S, :, DEC_T - 1:T_S:DEC_T], AX_X, ALU.add).then_inc(s("wss_done"), 1)
            dve.wait_ge(s("qg_done"), 1)
            for h in range(MH):
                TT(prod[:, h, :].rearrange("p (b t) -> p b t", t=DEC_T), qmT[:, h, T_P:T].rearrange("p (b t) -> p b t", t=DEC_T),
                   n_s[:, :, h].unsqueeze(2).broadcast_to([P, DEC_B, DEC_T]), ALU.mult).then_inc(s("prod_done"), 1)

        def state(u):
            wait(dve, "cup_done", u)
            new = ps[:, 4:6, 0:2 * W1]
            if u == 1:
                CP(Cst[:].rearrange("p (b h) v -> p b (h v)", b=2), new).then_inc(s("st_done"), 1)
                return
            dve.wait_ge(s("st_done"), u - 1)
            for h in range(MH):
                last = STT(out=Cst[:, h, :], in0=Cst[:, h, :], scalar=Gt[:, u % 2, h, P - 1:P],
                           in1=ps[:, 4 + h // 2, (h % 2) * W1:(h % 2 + 1) * W1], op0=ALU.mult, op1=ALU.add)
            last.then_inc(s("st_done"), 1)
            if u == NC:
                dve.wait_ge(s("st_done"), NC)
                CP(n_p[:], Cst[:, :, MD]).then_inc(s("np_done"), 1)

        def sample_state(r):
            h, hf_ = r // 2, r % 2
            half_b = slice(4 * hf_, 4 * hf_ + 4)
            step(CP(Cs[:, half_b, MD], n_s[:, half_b, h]))
            wait(dve, "rcup_done", r + 1)
            for bb in range(4):
                b = 4 * hf_ + bb
                last = STT(out=Cs[:, b, :], in0=Cs[:, b, :], scalar=dec_s[:, b, h:h + 1],
                           in1=ps[:, 4 + bb // 2, (bb % 2) * W1:(bb % 2 + 1) * W1], op0=ALU.mult, op1=ALU.add)
            step(last)
            CP(n_s[:, half_b, h], Cs[:, half_b, MD]).then_inc(s("round_upd"), 1)

        def num_view(n):
            return ps[0:n, 2:4, 0:2 * W1].rearrange("p b (h v) -> p b h v", v=W1)

        def h_denominator(u):
            c, _, n = unit_tokens(u)
            v = H_ORDER.index(u) + 1
            wait(dve, "num_done", v)
            CP(hden[0:n, :].rearrange("p (b h) -> p b h", b=2), num_view(n)[:, :, :, MD]).then_inc(s("hden_done"), 1)
            dve.wait_ge(s("hden_done"), v)
            step(STT(out=hab[0:n, :], in0=hden[0:n, :], scalar=-1.0, in1=hden[0:n, :], op0=ALU.mult, op1=ALU.max))
            step(TT(hab[0:n, :], hab[0:n, :], enm[0:n, c, :], ALU.max))
            wait(dve, "hf_ready", v - 1)
            step(V.reciprocal(hrd[0:n, :], hab[0:n, :]))

        def h_mean_square(u):
            _, _, n = unit_tokens(u)
            v = H_ORDER.index(u) + 1
            wait(dve, "sq_done", v)
            wait(dve, "h_done", v - 1)
            step(STT(out=hf[0:n, :], in0=hss[0:n, :], scalar=1.0 / MD, in1=hrd[0:n, :], op0=ALU.mult, op1=ALU.mult))
            TT(hf[0:n, :], hf[0:n, :], hrd[0:n, :], ALU.mult).then_inc(s("hq_ready"), 1)

        def h_scale(u):
            _, _, n = unit_tokens(u)
            v = H_ORDER.index(u) + 1
            wait(dve, "hf_ready", v)
            TT(hs[0:n, :, :].rearrange("p (b h) v -> p b h v", b=2), num_view(n)[:, :, :, 0:MD],
               hf[0:n, :].rearrange("p (b h) -> p b h", b=2).unsqueeze(3).broadcast_to([n, 2, 2, MD]), ALU.mult)\
                .then_inc(s("h_done"), 1)

        def hT_evac(u):
            _, off, n = unit_tokens(u)
            v = H_ORDER.index(u) + 1
            wait(dve, "hT_done", v)
            TT(qmT[:, :, off:off + n], ps[:, 1, 0:MH * n].rearrange("p (h t) -> p h t", h=MH),
               gmh[:].unsqueeze(2).broadcast_to([P, MH, n]), ALU.mult).then_inc(s("hT_evac"), 1)

        for it in range(S_P4 - S_P3):
            done = None
            if 2 <= it <= NC + 2:
                done = it - 1 if it <= NC + 1 else 0
                h_denominator(done)
            if 2 <= it <= NC + 1:
                state(it - 1)
            if done is not None:
                h_mean_square(done)
                h_scale(done)
            if it <= NC:
                q_gate(it)
                sd_mul(it)
            if it == 0:
                sample_extras()
            if 1 <= it <= N_ROUND:
                sample_state(it - 1)
            if done is not None:
                hT_evac(done)

        def gate_a(t):
            wait(dve, "za_used", t + 1)
            TT(qaT[:, t, :], qaT[:, t, :], zaT[:, t, :], ALU.mult).then_inc(s("ag_done"), 1)

        def a_lo(t):
            wait(dve, "ah_done", t + 1)
            TT(al[:, t * T:(t + 1) * T], qaT[:, t, :], ah[:, t * T:(t + 1) * T].bitcast(F32), ALU.subtract).then_inc(s("al_done"), 1)

        for m in range(NSUB - S_P4):
            sub = S_P4 + m
            _, kind, _, _, w = sub_of(sub)
            if m % 2 == 0 and m < 2 * G:
                gate_a(m // 2)
            if m % 2 == 1 and 3 <= m < 2 * G + 3:
                a_lo((m - 3) // 2)
            if kind == "zm":
                wait(dve, "sgz_ready", sub - 3 * FIRST["zm"] + 1)
                TT(sg[:, m % 2, 0:w], ps[:, 6 + sub % 2, 0:w], sg[:, m % 2, 0:w], ALU.mult).then_inc(s("proj_free"), 1)

        for j in range(MH):
            wait(dve, "mh_done", j + 1)
            TT(ml_[:, j * T:(j + 1) * T], qmT[:, j, :], mh_[:, j * T:(j + 1) * T].bitcast(F32), ALU.subtract)\
                .then_inc(s("ml_done"), 1)
        dve.wait_ge(s("gpost_ld"), 16)
        for t in range(NTILE):
            _, n = x_cols(t)
            y = y_out[0:n, t % 2, :]
            wait(dve, "rs_y", t + 1)
            if t >= 2:
                dve.wait_ge(s(f"y_st{t % 2}"), 16 * (t // 2))
            if t == 0:
                wait(dve, "sub_done", NSUB)
            ins = STT(out=y, in0=bank_pair(2 * (t % 4), n).rearrange("p b c -> p (b c)"), scalar=stat[0:n, NTILE + t:NTILE + t + 1],
                      in1=g_post_b[0:n, :], op0=ALU.mult, op1=ALU.mult)
            ins.then_inc(s("y_free"), 1)
            dve.wait_ge(s("y_free"), t + 1)
            dve.wait_ge(s(f"xr_ld{t % 2}"), 16 * (t // 2 + 1))
            TT(y, y, x_res[0:n, t % 2, :], ALU.add).then_inc(s("y_ready"), 1)

    @block.gpsimd
    def _(pool):
        Q = nc.gpsimd
        step = Step(pool, "pool_step")

        def rsqrt(dst, mean_sq):
            n, w = mean_sq.shape
            return Q.tensor_tensor(dst, mean_sq, half[0:n, 0:w], ALU.pow)

        step(Q.memset(half[:], -0.5))
        Q.memset(ones[:], 1.0)
        Q.memset(vm1[:, :, :, MD:W1], 1.0)
        Q.memset(xh[:, KT * T:XW].bitcast(F32), 0.0)
        Q.memset(xl[:, KT * T:XW].bitcast(F32), 0.0).then_inc(s("pads"), 1)

        Q.memset(gates[:], 0.0).then_inc(s("gates_zero"), 1)

        for t in range(NTILE):
            _, n = x_cols(t)
            wait(pool, "ss_ready", t + 1)
            r = stat[0:n, NTILE + t:NTILE + t + 1]
            step(Q.tensor_scalar(r, stat[0:n, t:t + 1], 1.0 / D, EPS, ALU.mult, ALU.add))
            rsqrt(r, r).then_inc(s("rstd_ready"), 1)
            if t == 1:
                wait(pool, "wt_hi_a", 2)
                Q.tensor_tensor(wt_lo[:, 4:6, :], wt_raw[:, 4:6, :], wt_hi[:, 4:6, :].bitcast(F32), ALU.subtract)\
                    .then_inc(s("wt_split_p"), 1)

        def split_lo(n):
            kind, j = SEQ[n]
            wait(pool, "w_hi", n + 1)
            hi, lo = (w_hi, w_lo) if kind == "in" else (wah, wal) if j < 4 else (wbh, wbl)
            q = j % 2 if kind == "in" else j % 4
            Q.tensor_tensor(lo[:, q, :], w_raw[:, n % 2, :], hi[:, q, :].bitcast(F32), ALU.subtract).then_inc(s("w_lo"), 1)

        split_lo(0)
        wait(pool, "tok_done", NTILE)
        Q.memset(rows[:], 0.0).then_inc(s("rows_zero"), 1)

        def splits(sub):
            for n in PLAN.get(sub, []):
                split_lo(n)

        for sub in range(S_P2 - 1):
            splits(sub)

        def normalise(u):
            b = u % 2
            wait(pool, "rden_done", u + 1)
            if u < 2 * NC:
                k0 = WIN if u < 2 else 0
                p = prob[:, b, :, k0:]
                Q.tensor_tensor(p, p, rden[:, b, :].unsqueeze(2).broadcast_to([P, G, 2 * WIN - k0]), ALU.mult)\
                    .then_inc(s("prob_ready"), 1)
            else:
                step(Q.tensor_tensor(prob_s[:], prob_s[:], rden[:, b, :].unsqueeze(2).broadcast_to([P, 4, KEYS_S]), ALU.mult))
                for q in range(4):
                    last = Q.tensor_tensor(new_s[:, q, :].rearrange("p (b t) -> p b t", t=DEC_T),
                                           prob_s[:, q, WIN:KEYS_S].unsqueeze(1).broadcast_to([P, DEC_B, DEC_T]),
                                           newmask[:, q % 2, :].unsqueeze(2).broadcast_to([P, DEC_B, DEC_T]), ALU.mult)
                last.then_inc(s("prob_ready"), 1)

        for it in range(S_P3 - S_P2):
            if 1 <= it <= N_ATT:
                normalise(it - 1)
            splits(S_P2 + it - 1)

        def masked_values(r):
            h, hf_ = r // 2, r % 2
            wait(pool, "rcup_done", r)
            if r == 0:
                wait(pool, "g_done", 1)
                wait(pool, "scored", N_ATT)
            Q.tensor_tensor(vmk[:], vm1[0:T_S, NC, h:h + 1, :].broadcast_to([T_S, 4, W1]),
                            seqsel[:, 4 * hf_:4 * hf_ + 4].unsqueeze(2).broadcast_to([T_S, 4, W1]), ALU.mult)\
                .then_inc(s("vmk_done"), 1)

        def h_factor(u):
            _, _, n = unit_tokens(u)
            v = H_ORDER.index(u) + 1
            wait(pool, "hq_ready", v)
            step(Q.tensor_scalar(hf[0:n, :], hf[0:n, :], EPS, None, ALU.add))
            step(rsqrt(hf[0:n, :], hf[0:n, :]))
            Q.tensor_tensor(hf[0:n, :], hf[0:n, :], hrd[0:n, :], ALU.mult).then_inc(s("hf_ready"), 1)

        for it in range(S_P4 - S_P3):
            if 2 <= it <= NC + 2:
                h_factor(it - 1 if it <= NC + 1 else 0)
            if it < N_ROUND:
                masked_values(it)
            splits(S_P3 + it)

        for m in range(NSUB - S_P4):
            sub = S_P4 + m
            _, kind, t, off, w = sub_of(sub)
            if m % 2 == 0 and m < 2 * G:
                q = m // 2
                wait(pool, "sgza_ready", q + 1)
                Q.tensor_tensor(zaT[:, q, :], zaT[:, q, :], sg_za[:, q % 2, :], ALU.mult).then_inc(s("za_used"), 1)
            if m == 2 * G:
                Q.memset(ah[:, MH * T:CW].bitcast(F32), 0.0)
                Q.memset(al[:, MH * T:CW].bitcast(F32), 0.0)
            wait(pool, "proj_free", sub + 1)
            x = qmT[:, t, off:off + w]
            Q.tensor_tensor(x, x, sg[:, m % 2, 0:w], ALU.mult).then_inc(s("sg_used"), 1)
            splits(sub)

        wait(pool, "sub_done", NSUB)
        Q.memset(mh_[:, MH * T:CW].bitcast(F32), 0.0)
        Q.memset(ml_[:, MH * T:CW].bitcast(F32), 0.0).then_inc(s("pads"), 1)
        for j in range(4, KT):
            split_lo(POS[("out", j)])
        for t in range(NTILE):
            _, n = x_cols(t)
            wait(pool, "ss_y", t + 1)
            r = stat[0:n, NTILE + t:NTILE + t + 1]
            step(Q.tensor_scalar(r, stat[0:n, t:t + 1], 1.0 / D, EPS, ALU.mult, ALU.add))
            rsqrt(r, r).then_inc(s("rs_y"), 1)

    block.__exit__(None, None, None)


OUTPUTS = [("y_prompt", (1, T_P, D)), ("y_sample", (DEC_B, DEC_T, D)),
           ("win_k_prompt", (1, 1, WIN, KVH, HD)), ("win_v_prompt", (1, 1, WIN, KVH, HD)),
           ("C_prompt", (1, 1, MH, MD, MD)), ("n_prompt_T", (MD, MH)), ("m_last_T", (MH, 1 + DEC_B)),
           ("win_k_sample", (1, DEC_B, WIN, KVH, HD)), ("win_v_sample", (1, DEC_B, WIN, KVH, HD)),
           ("C_sample", (1, DEC_B, MH, MD, MD)), ("n_sample_T", (MD, DEC_B, MH))]


def constants():
    f = np.float32
    tok = np.arange(P)
    slopes = (2.0 ** (-8.0 * (np.arange(AH) + 1) / AH)).astype(f)

    def bias(diff, slope):
        return np.where((diff >= 0) & (diff < WIN), -slope * diff.astype(f), f(NEG)).astype(f)

    diff = tok[:, None, None] + WIN - np.arange(2 * WIN)[None, None, :]
    bias_prompt = bias(diff, slopes[None, :, None])
    g, t = (tok // DEC_T) % G, tok % DEC_T
    bias_sample = np.stack([bias(t[:, None] + WIN - np.arange(KEYS_S)[None, :], slopes[kv * G + g][:, None])
                            for kv in range(KVH)], axis=1)
    st = np.arange(T_S)
    same = st[:, None] // DEC_T == st[None, :] // DEC_T
    resets = np.ones((MH, T), f)
    resets[:, 0:T_P:P] = 0
    resets[:, T_P::DEC_T] = 0
    own = np.arange(DEC_B)[None, None, :] == 4 * np.arange(2)[None, :, None] + (tok // 32)[:, None, None]
    return {"ident": np.eye(P, dtype=f),
            "chunk_mask": np.where(tok[:, None] > tok[None, :], f(NEG), f(0)),
            "seq_mask": np.where(same & (st[:, None] <= st[None, :]), f(0), f(NEG)),
            "bias_prompt": bias_prompt, "bias_sample": bias_sample, "resets": resets,
            "new_key_mask": own.astype(f),
            "seq_select": (st[:, None] // DEC_T == np.arange(DEC_B)[None, :]).astype(f)}


def kernel(**inputs):
    import concourse.bacc as bacc
    from concourse.bass_utils import run_bass_kernel_spmd

    a = {n: np.asarray(v) for n, v in inputs.items()}
    w_in, w_out = a["w_in"][0], a["w_out"][0]

    def pair_heads(off):
        cols = np.arange(AH * HD).reshape(KVH, G, HD).transpose(1, 0, 2).reshape(G, P)
        return [off + c for c in cols]

    tile_cols = [np.arange(C_KA, C_KA + KV_W)] + pair_heads(C_QA)
    for off in (C_KM, C_QM):
        tile_cols += [np.arange(off + P * t, off + P * (t + 1)) for t in range(MH)]
    tile_cols += pair_heads(C_ZA)
    for off in (C_OM, C_ZM):
        tile_cols += [np.arange(off + P * t, off + P * (t + 1)) for t in range(MH)]
    rows = w_in.reshape(KT, P, -1)
    w_in_tiles = np.stack([rows[:, :, c].transpose(1, 0, 2).reshape(P, KT * P) for c in tile_cols])
    tok_cols = np.concatenate([np.arange(C_VM, C_VM + 2 * MD), np.arange(C_VA, C_VA + VA0),
                               np.arange(C_VM + 2 * MD, C_VM + 4 * MD), np.arange(C_VA + VA0, C_VA + KV_W),
                               np.arange(C_G, C_G + 2 * MH)])
    w_tok = rows[:, :, tok_cols].transpose(1, 0, 2)
    w_out_tiles = np.concatenate([np.stack([w_out[c] for c in pair_heads(0)]), w_out[A_W:].reshape(MH, P, D)])
    sinks = a["attn_sinks"].reshape(KVH, G)
    rows_g = (np.arange(P) // DEC_T) % G
    arrays = {
        "x_prompt": a["x_prompt"], "x_sample": a["x_sample"], "g_pre": a["g_pre"], "g_post": a["g_post"],
        "w_tok": w_tok, "w_in_tiles": w_in_tiles, "w_out_tiles": w_out_tiles,
        "cache_win_k": a["cache_win_k"], "cache_win_v": a["cache_win_v"],
        "cache_k_T": a["cache_win_k"][0].transpose(2, 3, 0, 1).reshape(P, DEC_B, WIN),
        "state_C": a["state_C"], "state_n_T": a["state_n"][0].transpose(2, 0, 1), "state_m_T": a["state_m"][0].T,
        "b_gate": a["b_gate"].reshape(2 * MH, 1), "g_mh_T": a["g_mh"][0].T,
        "sinks_prompt": np.broadcast_to(a["attn_sinks"], (P, AH)),
        "sinks_sample": np.stack([sinks[q // 2][rows_g] for q in range(4)], axis=1),
        **constants(),
    }
    arrays = {n: np.ascontiguousarray(v) for n, v in arrays.items()}
    nc = bacc.Bacc("TRN2", target_bir_lowering=False, num_devices=1)
    ins = {n: nc.dram_tensor(f"in_{n}", v.shape, mybir.dt.from_np(v.dtype), kind="ExternalInput").ap()
           for n, v in arrays.items()}
    outs = {n: nc.dram_tensor(f"out_{n}", shape, F32, kind="ExternalOutput").ap() for n, shape in OUTPUTS}
    build(nc, ins, outs)
    r = run_bass_kernel_spmd(nc, [{f"in_{n}": v for n, v in arrays.items()}], core_ids=[0]).results[0]
    got = {n: np.asarray(r[f"out_{n}"]) for n, _ in OUTPUTS}
    got["n_prompt_T"] = np.ascontiguousarray(got["n_prompt_T"].T).reshape(1, 1, MH, MD)
    got["n_sample_T"] = np.ascontiguousarray(got["n_sample_T"].transpose(1, 2, 0)).reshape(1, DEC_B, MH, MD)
    m_last = got["m_last_T"]
    got["m_last_T"] = np.ascontiguousarray(m_last[:, 0]).reshape(1, 1, MH)
    return tuple(got[n] for n, _ in OUTPUTS) + (np.ascontiguousarray(m_last[:, 1:].T).reshape(1, DEC_B, MH),)
```

```python
import numpy as np
import concourse.bass as bass
from concourse import mybir

F32 = mybir.dt.float32
F32R = mybir.dt.float32r
ALU = mybir.AluOpType
ACT = mybir.ActivationFunctionType
AX_X = mybir.AxisListType.X

P = 128
D = 1024
KT = D // P
T_P, DEC_B, DEC_T = 1024, 8, 8
T_S = DEC_B * DEC_T
T = T_P + T_S
NC = T_P // P
NTILE = NC + 1
AH, KVH, HD = 8, 2, 64
G = AH // KVH
WIN = 128
MH, MD = 4, 128
EPS = 1e-6
NEG = -1e30
PQ = 32
A_W, KV_W, M_W = AH * HD, KVH * HD, MH * MD
KEYS_S = WIN + DEC_T
W1 = MD + 1

C_QA, C_KA = 0, A_W
C_VA = C_KA + KV_W
C_ZA = C_VA + KV_W
C_QM = C_ZA + A_W
C_KM, C_VM, C_OM, C_ZM = (C_QM + i * M_W for i in range(1, 5))
C_G = C_ZM + M_W

SUBS = [(0, 364), (364, 364), (728, 360)]
TILES = ["ka"] + ["qa"] * 4 + ["km"] * 4 + ["qm"] * 4 + ["za"] * 4 + ["om"] * 4 + ["zm"] * 4
FIRST = {"ka": 0, "qa": 1, "km": 5, "qm": 9, "za": 13, "om": 17, "zm": 21}
NJ = len(TILES)
NSUB = 3 * NJ
S_P2, S_P3, S_P4 = 3 * FIRST["km"], 3 * FIRST["za"], 3 * FIRST["om"]
UNIT_HEADS = np.arange(AH).reshape(KVH, 2, G // 2).transpose(1, 0, 2).reshape(AH)
TOK_W = 648
TOK_H = TOK_W // 2
VA0 = TOK_H - 2 * MD


def inter_quarter(j, half):
    return (j + half) % 4


def weight_sequence():
    seq = []
    for j in range(NJ):
        seq.append(("in", j))
        if j >= NJ - 4:
            seq.append(("out", j - (NJ - 4)))
    return seq + [("out", k) for k in range(4, KT)]


SEQ = weight_sequence()
POS = {item: n for n, item in enumerate(SEQ)}


def split_plan():
    plan = {-1: [POS[("in", 0)]]}
    for j in range(NJ - 1):
        plan.setdefault(3 * j, []).append(POS[("in", j + 1)])
    for k in range(4):
        plan[3 * (NJ - 5 + k) + 2] = [POS[("out", k)]]
    return plan


PLAN = split_plan()


def build(nc, i, o):
    base = 16512
    XW, CW = KT * T, MH * T
    sizes = [("A", 2 * 4 * XW), ("H", 6 * 4096), ("K", 3328), ("B", 16 * T), ("E", 4 * NTILE * MH * W1),
             ("D", 16 * T), ("C", 16 * T), ("F", 16 * T), ("GI", 27072)]
    off, at = base, {}
    for name, size in sizes:
        at[name] = off
        off += (size + 31) // 32 * 32
    end = off

    def sb(name, shape, dt, offset):
        return nc.alloc_sbuf_tensor_at(name, shape, dt, offset=offset)

    A, H, B, C, Dr, E, Fr, GI = (at[k] for k in ("A", "H", "B", "C", "D", "E", "F", "GI"))
    x_hl = sb("x_hl", [P, 2, XW], F32R, A)
    x_hl_s = sb("x_hl_s", [P, KT, 2, T_S], F32R, GI + 12288)
    xh, xl = x_hl[:, 0, :], x_hl[:, 1, :]
    w_raw = sb("w_raw", [P, 2, 1024], F32, H)
    w_hi = sb("w_hi", [P, 2, 1024], F32R, H + 8192)
    w_lo = sb("w_lo", [P, 2, 1024], F32R, H + 16384)
    qaT = sb("qaT", [P, G, T], F32, B)
    vm1 = sb("vm1", [P, NTILE, MH, W1], F32, E)
    kmT = sb("kmT", [P, MH, T], F32, Dr)
    qmT = sb("qmT", [P, MH, T], F32, C)
    zaT = sb("zaT", [P, G, T], F32, Fr)
    kaT = sb("kaT", [P, T], F32, GI)
    va = sb("va", [P, NTILE, KV_W], F32, GI + 4352)
    k = [at["K"]]

    def small(name, shape, dt=F32):
        n = int(np.prod(shape[1:])) * 4
        t = sb(name, shape, dt, k[0])
        k[0] += (n + 31) // 32 * 32
        assert k[0] <= at["B"], (name, k[0] - at["B"])
        return t

    ident = small("ident", [P, P])
    causal = small("causal", [P, P])
    causal_s = small("causal_s", [T_S, T_S])
    r1c = small("r1c", [P, NTILE, MH])
    r2c = small("r2c", [P, NTILE, MH])
    enm = small("enm", [P, NTILE, MH])
    glc = small("glc", [T_S, MH])
    mpb = small("mpb", [P, NC, MH])
    dec_s = small("dec_s", [P, DEC_B, MH])
    n_s = small("n_s", [P, DEC_B, MH])
    gmh = small("gmh", [P, MH])
    sink_p = small("sink_p", [P, AH])
    sink_s = small("sink_s", [P, 4])
    seqsel = small("seqsel", [T_S, DEC_B])
    inter_msk = small("inter_msk", [P, 2])
    inter_sel = small("inter_sel", [P, T_S])
    newmask = small("newmask", [P, 2, DEC_B])
    stat_2 = small("stat_2", [P, 1])
    stat = small("stat", [P, 2 * NTILE])
    minus_half = small("minus_half", [P, 4])
    ones = small("ones", [P, 1])
    x_raw = sb("x_raw", [P, 4, D], F32, B)
    wt_raw = sb("wt_raw", [P, KT, TOK_W], F32, H)
    wt_hi = sb("wt_hi", [P, KT, TOK_W], F32R, Dr)
    wt_lo = sb("wt_lo", [P, KT, TOK_W], F32R, Dr + 4 * KT * TOK_W)
    g_pre_b = sb("g_pre_b", [P, D], F32, Dr + 8 * KT * TOK_W)
    junk = sb("junk", [P, D], F32, Dr + 8 * KT * TOK_W + 4096)
    tok_lo = sb("tok_lo", [T_S, 2, TOK_H], F32, Dr + 8 * KT * TOK_W + 4096)
    gates = sb("gates", [P, NTILE, 2 * PQ], F32, GI + 9984)
    row = [sb(f"row{n}", [MH, T], F32, Dr + n * 4 * T) for n in range(6)]
    ib, fb, ra, rb, rc, rd = row
    NR = 3 * PQ + MH
    rows = sb("rows", [NR, T], F32, Dr + 6 * 4 * T)
    re_, rf, r_m, r_gl = (rows[q * PQ:q * PQ + MH, :] for q in range(4))
    P1S = Dr + 8 * KT * TOK_W + 8192
    resets = sb("resets", [MH, T], F32, Fr)
    bgi = sb("bgi", [MH, 1], F32, P1S)
    bgf = sb("bgf", [PQ + MH, 1], F32, P1S + 32)
    m0T = sb("m0T", [MH, DEC_B], F32, P1S + 64)
    mp = sb("mp", [MH, NC + DEC_B], F32, P1S + 128)
    m_last = sb("m_last", [MH, 1 + DEC_B], F32, P1S + 384)
    mpd = sb("mpd", [MH, NC, MH], F32, P1S + 256)
    bias_p = sb("bias_p", [P, AH, 2 * WIN], F32, GI + 17408)
    bias_s = sb("bias_s", [P, KVH, KEYS_S], F32, GI + 25600)
    kcT = sb("kcT", [P, DEC_B, KEYS_S], F32, GI + 8960)
    vc = sb("vc", [P, DEC_B, KV_W], F32, GI + 8960 + 4352)
    prob = sb("prob", [P, 2, G, 2 * WIN], F32, Fr)
    probT = sb("probT", [P, 2, 2, G * WIN], F32, Fr + 8192)
    qs = sb("qs", [P, DEC_B, G * DEC_T], F32, Fr + 16384)
    prob_s = sb("prob_s", [P, 4, KEYS_S], F32, Fr)
    new_s = sb("new_s", [P, 4, T_S], F32, Fr + 2560)
    k_out = sb("k_out", [P, 2, KV_W], F32, Fr + 4096)
    mx = small("mx", [P, 2, 4])
    nmx = small("nmx", [P, 2, 4])
    sd = small("sd", [P, 2, 4])
    den = small("den", [P, 2, 4])
    rden = small("rden", [P, 2, 4])
    n = GI
    Gt = sb("Gt", [P, 2, MH, P], F32, n)
    DT = sb("DT", [P, MH, P], F32, n + 4096)
    SD = sb("SD", [P, MH, P], F32, n + 6144)
    kw = sb("kw", [P, MH, P], F32, n + 8192)
    hs = sb("hs", [P, MH, P], F32, n + 10240)
    Cst = sb("Cst", [P, MH, W1], F32, n + 12288)
    Cs = sb("Cs", [P, DEC_B, W1], F32, n + 14368)
    vmk = sb("vmk", [T_S, 4, W1], F32, n + 18496)
    kws = sb("kws", [T_S, MH, P], F32, n + 20576)
    SDs = sb("SDs", [T_S, MH, T_S], F32, n + 22624)
    ITs = sb("ITs", [P, MH, W1], F32, n + 23648)
    hden = small("hden", [P, 4])
    hab = small("hab", [P, 4])
    hrd = small("hrd", [P, 4])
    hss = small("hss", [P, 4])
    hf = small("hf", [P, 4])
    wss = small("wss", [T_S, MH])
    n_p = small("n_p", [P, MH])
    a_hl = sb("a_hl", [P, 2, CW], F32R, E)
    ah, al = a_hl[:, 0, :], a_hl[:, 1, :]
    assert 8 * CW <= C - E
    wah = sb("wah", [P, 4, D], F32R, Fr)
    wal = sb("wal", [P, 4, D], F32R, Fr + 16384)
    sg_za = sb("sg_za", [P, 2, T], F32, Fr + 32768)
    sg = sb("sg", [P, 2, 364], F32, Fr + 32768 + 8 * T)
    assert Fr + 32768 + 8 * T + 8 * 364 <= end
    o_hl_s = sb("o_hl_s", [P, KT, 2, T_S], F32R, B + 12288)
    m_hl = sb("m_hl", [P, 2, CW], F32R, A)
    mh_, ml_ = m_hl[:, 0, :], m_hl[:, 1, :]
    wbh = sb("wbh", [P, 4, D], F32R, A + 8 * CW)
    wbl = sb("wbl", [P, 4, D], F32R, A + 8 * CW + 16384)
    x_res = sb("x_res", [P, 2, D], F32, H + 8192)
    y_out = sb("y_out", [P, 2, D], F32, H + 16384)
    g_post_b = sb("g_post_b", [P, D], F32, B)
    y_lo = sb("y_lo", [T_S, D], F32, B + 8192)
    junk5 = sb("junk5", [P, D], F32, B + 4096)

    ps = nc.alloc_psum_tensor("ps", [P, 8, 512], F32)
    sems = {}

    def s(name):
        if name not in sems:
            sems[name] = nc.alloc_semaphore(name)
        return sems[name]

    class Step:

        def __init__(self, eng, name):
            self.eng, self.sem, self.n = eng, s(name), 0

        def __call__(self, ins):
            self.n += 1
            ins.then_inc(self.sem, 1)
            self.eng.wait_ge(self.sem, self.n)

    def wait(eng, name, value):
        if value > 0:
            eng.wait_ge(s(name), value)

    def x_cols(t):
        return P * t, P if t < NC else T_S

    def kx(part, off, width):
        return part[:, 0:KT * T].rearrange("p (k t) -> p k t", k=KT)[:, :, off:off + width]

    def bank_pair(b, n, width=512):
        return ps[0:n, b:b + 2, 0:width]

    IT0 = 320

    COL_GROUPS = [(slice(0, 5), P), (slice(5, NC), P), (slice(NC, NTILE), T_S)]

    def row_cols(q, cs, n):
        c0 = 5 * (cs.start // 5)
        return ps[0:n, c0 // 5, 0:5 * NR].rearrange("p (c r) -> p c r", r=NR)[:, cs.start - c0:cs.stop - c0, q * PQ:q * PQ + MH]

    def sub_of(sub):
        j, (off, w) = sub // 3, SUBS[sub % 3]
        kind = TILES[j]
        return j, kind, j - FIRST[kind], off, w

    def unit_tokens(u):
        return (NC, T_P, T_S) if u == 0 else (u - 1, P * (u - 1), P)

    H_ORDER = list(range(1, NC + 1)) + [0]
    Y_ORDER = list(range(NC - 1)) + [NC, NC - 1]
    N_ATT = 2 * NC + 1
    N_ROUND = 2 * MH

    def split_lo(eng, engine, n):
        kind, j = SEQ[n]
        wait(eng, "w_hi", n + 1)
        wait(eng, "w_lo", n)
        hi, lo = (w_hi, w_lo) if kind == "in" else (wah, wal) if j < 4 else (wbh, wbl)
        q = j % 2 if kind == "in" else j % 4
        engine.tensor_tensor(lo[:, q, :], w_raw[:, n % 2, :], hi[:, q, :].bitcast(F32), ALU.subtract).then_inc(s("w_lo"), 1)

    block = nc.Block()
    block.__enter__()

    @block.sync
    def _(sp):
        def load_x(t):
            _, n = x_cols(t)
            wait(sp, "xT_done", t - 3)
            src = i["x_prompt"][0, P * t:P * (t + 1), :] if t < NC else i["x_sample"].rearrange("b t d -> (b t) d")
            sp.dma_start(x_raw[0:n, t % 4, :], src).then_inc(s(f"x_ld{t % 4}"), 16)

        def load_wt(g):
            sp.dma_start(wt_raw[:, 2 * g:2 * g + 2, :], i["w_tok"][:, 2 * g:2 * g + 2, :]).then_inc(s(f"wt_ld{g}"), 16)

        load_x(0)
        sp.dma_start(ident[:], i["ident"]).then_inc(s("ident_ld"), 16)
        sp.dma_start(g_pre_b[:], i["g_pre"].partition_broadcast(P).rearrange("p a d -> p (a d)")).then_inc(s("gpre_ld"), 16)
        load_wt(0)
        load_x(1)
        load_wt(1)
        load_wt(2)
        load_wt(3)
        load_x(2)
        load_x(3)
        misc = [(inter_msk[:], i["inter_mask"]), (inter_sel[:], i["inter_select"]),
                (causal[:], i["chunk_mask"]), (causal_s[:], i["seq_mask"]), (gmh[:], i["g_mh_T"]),
                (sink_p[:], i["sinks_prompt"]), (sink_s[:], i["sinks_sample"]),
                (seqsel[:], i["seq_select"]), (newmask[:], i["new_key_mask"]), (n_s[:], i["state_n_T"]),
                (bgi[:], i["b_gate"][0:MH, :]), (bgf[PQ:PQ + MH, :], i["b_gate"][MH:2 * MH, :]), (m0T[:], i["state_m_T"])]
        for dst, src in misc:
            sp.dma_start(dst, src).then_inc(s("misc_ld"), 16)
        for t in range(4, NTILE):
            load_x(t)

        def load_w(n):
            wait(sp, "w_lo", n - 1)
            kind, j = SEQ[n]
            sp.dma_start(w_raw[:, n % 2, :], i["w_in_tiles"][j] if kind == "in" else i["w_out_tiles"][j]).then_inc(s(f"w_ld{n % 2}"), 16)

        wait(sp, "wt_split_d", 3)
        wait(sp, "wt_split_p", 3)
        load_w(0)
        load_w(1)
        wait(sp, "tok_done", NTILE)
        sp.dma_start(resets[:], i["resets"]).then_inc(s("resets_ld"), 16)
        wait(sp, "rows_ps", 1)
        sp.dma_start(kcT[:, :, 0:WIN], i["cache_k_T"]).then_inc(s("att_ld"), 16)
        sp.dma_start(vc[:], i["cache_win_v"][0].rearrange("b w k d -> w b (k d)")).then_inc(s("att_ld"), 16)
        sp.dma_start(bias_p[:], i["bias_prompt"]).then_inc(s("att_ld"), 16)
        sp.dma_start(bias_s[:], i["bias_sample"]).then_inc(s("att_ld"), 16)
        for name, cache in (("win_k_sample", "cache_win_k"), ("win_v_sample", "cache_win_v")):
            sp.dma_start(o[name][0, :, 0:WIN - DEC_T].rearrange("b w k d -> b (w k d)"),
                         i[cache][0, :, DEC_T:WIN].rearrange("b w k d -> b (w k d)")).then_inc(s("out"), 16)
        load_w(2)
        wait(sp, "rows_done", 1)
        sp.dma_start(o["m_last_T"], m_last[:]).then_inc(s("m_out"), 16)

        def load_c(r):
            h, bs = r // 2, slice(4 * (r % 2), 4 * (r % 2) + 4)
            if r >= 2:
                sp.wait_ge(s(f"c_st{r % 2}"), 16 * h)
            sp.dma_start(Cs[:, bs, 0:MD], i["state_C"][0, bs, h].rearrange("b d v -> d b v")).then_inc(s(f"c_ld{r % 2}"), 16)

        def store_c(r):
            h, bs = r // 2, slice(4 * (r % 2), 4 * (r % 2) + 4)
            wait(sp, "round_upd", r + 1)
            sp.dma_start(o["C_sample"][0, bs, h].rearrange("b d v -> d b v"), Cs[:, bs, 0:MD]).then_inc(s(f"c_st{r % 2}"), 16)

        for n in range(3, len(SEQ)):
            kind, j = SEQ[n]
            if (kind, j) == ("in", FIRST["km"] + 2):
                sp.dma_start(o["win_v_prompt"].rearrange("a b w k d -> w (a b k d)"), va[:, NC - 1, :]).then_inc(s("v_out"), 16)
                sp.dma_start(o["win_v_sample"][0, :, WIN - DEC_T:WIN].rearrange("b t k d -> b t (k d)"),
                             va[0:T_S, NC, :]).then_inc(s("v_out"), 16)
            if (kind, j) == ("in", FIRST["za"] + 1):
                wait(sp, "ko_evac", 1)
                sp.dma_start(o["win_k_prompt"].rearrange("a b w k d -> w (a b k d)"), k_out[:, 0, :]).then_inc(s("k_outd"), 16)
                sp.dma_start(o["win_k_sample"][0, :, WIN - DEC_T:WIN].rearrange("b t k d -> b t (k d)"),
                             k_out[0:T_S, 1, :]).then_inc(s("k_outd"), 16)
                wait(sp, "pv_done", N_ATT)
                wait(sp, "scored", N_ATT)
                load_c(0)
                load_c(1)
            if (kind, j) == ("in", FIRST["za"] + 3):
                for r in range(2):
                    store_c(r)
                    load_c(r + 2)
            if (kind, j) == ("in", FIRST["om"]):
                for r in range(2, N_ROUND):
                    store_c(r)
                    if r + 2 < N_ROUND:
                        load_c(r + 2)
                sp.dma_start(o["n_sample_T"], n_s[:]).then_inc(s("out"), 16)
                wait(sp, "st_done", NC)
                sp.dma_start(o["C_prompt"].rearrange("a b h d v -> d (a b h) v"), Cst[:, :, 0:MD]).then_inc(s("cp_st"), 16)
                wait(sp, "np_done", 1)
                sp.dma_start(o["n_prompt_T"], n_p[:]).then_inc(s("cp_st"), 16)
            load_w(n)

        def load_res(p):
            t = Y_ORDER[p]
            _, n = x_cols(t)
            wait(sp, "y_ready", p - 1)
            src = i["x_prompt"][0, P * t:P * (t + 1), :] if t < NC else i["x_sample"].rearrange("b t d -> (b t) d")
            sp.dma_start(x_res[0:n, p % 2, :], src).then_inc(s(f"xr_ld{p % 2}"), 16)

        wait(sp, "ag_done", G)
        wait(sp, "ah_done", G)
        sp.dma_start(g_post_b[:], i["g_post"].partition_broadcast(P).rearrange("p a d -> p (a d)")).then_inc(s("gpost_ld"), 16)
        wait(sp, "sub_done", NSUB)
        load_res(0)
        load_res(1)
        for p, t in enumerate(Y_ORDER):
            _, n = x_cols(t)
            dst = o["y_prompt"][0, P * t:P * (t + 1), :] if t < NC else o["y_sample"].rearrange("b t d -> (b t) d")
            for q, cols in enumerate([slice(0, D)] if p < NTILE - 1 else [slice(0, 512), slice(512, D)]):
                wait(sp, "y_ready", p + 1 + q)
                sp.dma_start(dst[:, cols], y_out[0:n, p % 2, cols]).then_inc(s(f"y_st{p % 2}"), 16)
            if p + 2 < NTILE:
                load_res(p + 2)
        sp.wait_ge(s("y_st0"), 16 * 6)
        sp.wait_ge(s("y_st1"), 16 * 4)
        sp.wait_ge(s("out"), 16 * 3)
        sp.wait_ge(s("m_out"), 16)
        sp.wait_ge(s("v_out"), 32)
        sp.wait_ge(s("k_outd"), 32)
        sp.wait_ge(s("c_st0"), 16 * MH)
        sp.wait_ge(s("c_st1"), 16 * MH)
        sp.wait_ge(s("cp_st"), 32)

    @block.tensor
    def _(pe):
        mm = nc.tensor.matmul
        state = {"sub": 0, "at": 0}

        def split_products(out, hl, hl_s, wh, wl, first, final):
            n = hl.shape[2]
            if n == P:
                mm(out, hl[:, 0, :], wh, start=first, stop=False, skip_group_check=True)
                mm(out, hl[:, 0, :], wl, start=False, stop=False, skip_group_check=True)
                return mm(out, hl[:, 1, :], wh, start=False, stop=final, skip_group_check=True)
            mm(out, hl_s.rearrange("p a t -> p (a t)"), wh, start=first, stop=False, skip_group_check=True)
            return mm(out[0:n], hl[:, 0, :], wl, start=False, stop=final, skip_group_check=True)

        def x_transpose(t):
            off, n = x_cols(t)
            b = 2 * (t % 2)
            wait(pe, "x_split", t - 1)
            if t == 0:
                pe.wait_ge(s("ident_ld"), 16)
            for kk in range(KT):
                if kk == 0:
                    wait(pe, "xn_ready", t + 1 if t else 0)
                    wait(pe, "xn_half", 0 if t else 1)
                if kk == 4 and t == 0:
                    last.then_inc(s("xT_half"), 1)
                    wait(pe, "xn_ready", 1)
                last = nc.tensor.transpose(ps[:, b + kk // 4, (kk % 4) * P:(kk % 4) * P + n],
                                           x_raw[0:n, t % 4, kk * P:(kk + 1) * P], ident[0:n, 0:n])
            last.then_inc(s("xT_done"), 1)

        def token_major(t, ks):
            off, n = x_cols(t)
            b = 4 + 2 * (t % 2)
            wait(pe, "x_split", t + 1)
            wait(pe, "tok_act", t - 1)
            wait(pe, "tok_dve", t - 1)
            if t == 0:
                wait(pe, "ones_ready", 1)
            if t == NC:
                wait(pe, "xs_ready", 1)
            for kk in ks:
                if t == 0:
                    wait(pe, "wt_split_d", [0, 1, 2, 0, 0, 0, 3, 0][kk])
                    wait(pe, "wt_split_p", [1, 0, 0, 0, 2, 3, 0, 0][kk])
                for q in range(2):
                    last = split_products(ps[:, b + q, 0:TOK_H], x_hl[:, :, kk * T + off:kk * T + off + n], x_hl_s[:, kk],
                                          *(w[:, kk, q * TOK_H:(q + 1) * TOK_H] for w in (wt_hi, wt_lo)),
                                          first=(kk == 0), final=(kk == KT - 1))
            if ks[-1] == KT - 1:
                last.then_inc(s("tok_done"), 1)

        def project(n):
            for _ in range(n):
                sub, at_ = state["sub"], state["at"]
                j, kind, _, off, w = sub_of(sub)
                if at_ == 0:
                    if sub < 2:
                        wait(pe, "tok_act", NC)
                        wait(pe, "tok_dve", NC)
                    else:
                        wait(pe, "proj_free", sub - 1)
                    if sub % 3 == 0:
                        wait(pe, "w_lo", POS[("in", j)] + 1)
                kk, pas = at_ // 3, at_ % 3
                wt = (w_lo if pas == 2 else w_hi)[:, j % 2, kk * P:(kk + 1) * P]
                xt = (xl if pas == 1 else xh)[:, kk * T + off:kk * T + off + w]
                last = mm(ps[:, 6 + sub % 2, 0:w], wt, xt, start=(at_ == 0), stop=(at_ == 23))
                state["at"] += 1
                if state["at"] == 24:
                    last.then_inc(s("sub_done"), 1)
                    state["sub"], state["at"] = sub + 1, 0

        x_transpose(0)
        for t in range(NTILE):
            if t < 2:
                token_major(t, range(0, KT // 2))
                x_transpose(t + 1)
                token_major(t, range(KT // 2, KT))
                continue
            if t + 1 < NTILE:
                x_transpose(t + 1)
            token_major(t, range(KT))

        project(24)
        wait(pe, "tok_dve", NTILE)
        wait(pe, "tok_act", NTILE)
        wait(pe, "x_split", NTILE)
        for c in range(NTILE):
            _, n = x_cols(c)
            last = nc.tensor.transpose(ps[0:PQ + MH, c // 4, (c % 4) * P:(c % 4) * P + n], gates[0:n, c, 0:PQ + MH], ident[0:n, 0:n])
        last.then_inc(s("rows_ps"), 1)
        project(24 * 8)
        wait(pe, "rows_done", 1)
        for c in range(NTILE):
            off, n = x_cols(c)
            nc.tensor.transpose(ps[0:n, c // 5, (c % 5) * NR:(c % 5 + 1) * NR], rows[:, off:off + n], ident[0:NR, 0:NR])
        mm(ps[:, 2, 0:NC * MH], ones[0:MH, 0:1].broadcast_to([MH, P]), mpd[:].rearrange("k c h -> k (c h)"), start=True, stop=True)\
            .then_inc(s("cols_ps"), 1)
        project(24 * S_P2 - 24 * 9)

        def scores(u):
            wait(pe, "scored", u)
            if u == 0:
                wait(pe, "proj_free", S_P2 - 2)
                wait(pe, "cols_done", 1)
            if u < 2 * NC:
                blk, pair = u // 2, u % 2
                k0 = 1 if blk == 0 else 0
                for g in range(2):
                    for kv in range(KVH):
                        rows = slice(kv * HD, (kv + 1) * HD)
                        last = mm(ps[:, kv, g * 256 + k0 * WIN:g * 256 + 256],
                                  qaT[rows, 2 * pair + g, blk * P:(blk + 1) * P],
                                  kaT[rows, (blk - 1 + k0) * P:(blk + 1) * P], start=True, stop=True)
            else:
                wait(pe, "qs_ready", 1)
                for b in range(DEC_B):
                    r = 32 * (b % 4)
                    for kv in range(KVH):
                        rows = slice(kv * HD, (kv + 1) * HD)
                        last = mm(ps[r:r + 32, kv, (b // 4) * KEYS_S:(b // 4 + 1) * KEYS_S], qs[rows, b, :], kcT[rows, b, :],
                                  start=True, stop=True)
            last.then_inc(s("qk_done"), 1)

        def prob_transposes(u):
            wait(pe, "prob_ready", u + 1)
            wait(pe, "pT_act", u)
            wait(pe, "pT_dve", u - 2)
            if u < 2 * NC:
                for kb in range(1 if u < 2 else 0, 2):
                    for g in range(G):
                        last = nc.tensor.transpose(ps[:, 2 + kb, g * P:(g + 1) * P],
                                                   prob[:, u % 2, g, kb * WIN:(kb + 1) * WIN], ident[:])
            else:
                for q in range(4):
                    nc.tensor.transpose(ps[:, 2, q * P:(q + 1) * P], prob_s[:, q, 0:WIN], ident[:])
                for q in range(4):
                    last = nc.tensor.transpose(ps[0:T_S, 3, q * P:(q + 1) * P], new_s[:, q, :], ident[:])
            last.then_inc(s("pTr_done"), 1)

        def values(u):
            wait(pe, "pT_act", u + 1)
            wait(pe, "pT_dve", u - 1)
            wait(pe, "att_out", u - 1)
            if u < 2 * NC:
                blk = u // 2
                for kb in range(1 if blk == 0 else 0, 2):
                    for kv in range(KVH):
                        rows = slice(kv * HD, (kv + 1) * HD)
                        last = mm(ps[rows, 4 + u % 2, 0:2 * P], va[:, blk - 1 + kb, rows],
                                  probT[:, u % 2, kb, kv * 2 * P:(kv + 1) * 2 * P],
                                  start=(kb == 0 or blk == 0), stop=(kb == 1), skip_group_check=True)
            else:
                for kv in range(KVH):
                    rows = slice(kv * HD, (kv + 1) * HD)
                    mm(ps[rows, 4, 0:2 * P], va[0:T_S, NC, rows], probT[0:T_S, 0, 1, kv * 2 * P:(kv + 1) * 2 * P],
                       start=True, stop=False, skip_group_check=True)
                for b in range(DEC_B):
                    for kv in range(KVH):
                        rows = slice(kv * HD, (kv + 1) * HD)
                        last = mm(ps[rows, 4, b * 32:(b + 1) * 32], vc[:, b, rows],
                                  probT[:, 0, 0, kv * 2 * P + b * 32:kv * 2 * P + (b + 1) * 32],
                                  start=False, stop=(b == DEC_B - 1), skip_group_check=True)
            last.then_inc(s("pv_done"), 1)

        for it in range(S_P3 - S_P2):
            if it < N_ATT:
                scores(it)
            project(24)
            if 1 <= it <= N_ATT:
                prob_transposes(it - 1)
            if 2 <= it <= N_ATT + 1:
                values(it - 2)
            if it == N_ATT + 1:
                nc.tensor.transpose(ps[:, 0, 0:P], kaT[:, T_P - P:T_P], ident[:])
                nc.tensor.transpose(ps[0:T_S, 0, P:2 * P], kaT[:, T_P:T], ident[:]).then_inc(s("ko_ps"), 1)

        def log_weights(u):
            c, off, n = unit_tokens(u)
            wait(pe, "kw_done", u)
            if u == 0:
                wait(pe, "ko_evac", 1)
                for h in range(MH):
                    nc.tensor.transpose(ps[:, 0, 256 + h * n:256 + (h + 1) * n], glc[:, h:h + 1].broadcast_to([n, P]), ident[0:n, 0:n])
            for h in range(MH):
                last = nc.tensor.transpose(ps[0:n, 0, h * n:(h + 1) * n], r1c[0:n, c, h:h + 1].broadcast_to([n, n]), ident[0:n, 0:n])
            last.then_inc(s("r1_done"), 1)

        def m_scores(u):
            _, off, n = unit_tokens(u)
            wait(pe, "sd_done", u)
            wait(pe, "hT_evac", u - 2)
            if u == 0:
                wait(pe, "proj_free", S_P3)
            for h in range(MH):
                last = mm(ps[0:n, 1, h * n:(h + 1) * n], kmT[:, h, off:off + n], qmT[:, h, off:off + n], start=True, stop=True)
            last.then_inc(s("s_done"), 1)

        def k_transposes(u):
            _, off, n = unit_tokens(u)
            wait(pe, "mask_done", u + 1)
            for h in range(MH):
                last = nc.tensor.transpose(ps[0:n, 0, h * P:(h + 1) * P], kmT[:, h, off:off + n], ident[:])
            last.then_inc(s("kT_done"), 1)

        def numerator(u):
            c, off, n = unit_tokens(u)
            v = H_ORDER.index(u) + 1
            wait(pe, "sd_done", u + 1)
            wait(pe, "qg_done", u + 1)
            wait(pe, "h_done", v - 1)
            if u == 0:
                wait(pe, "it_evac", N_ROUND)
            else:
                wait(pe, "st_done", u - 1)
            for h in range(MH):
                out = ps[0:n, 2 + h // 2, (h % 2) * W1:(h % 2 + 1) * W1]
                last = mm(out, (SD if u else SDs)[0:n, h, :], vm1[0:n, c, h, :], start=True, stop=(u == 1), skip_group_check=True)
                if u > 1:
                    last = mm(out, qmT[:, h, off:off + n], Cst[:, h, :], start=False, stop=True, skip_group_check=True)
                if u == 0:
                    last = mm(out, inter_sel[:], ITs[:, h, :], start=False, stop=True, skip_group_check=True)
            last.then_inc(s("num_done"), 1)

        def state_update(u):
            c, _, _ = unit_tokens(u)
            wait(pe, "kw_done", u + 1)
            wait(pe, "round_upd", min(u, N_ROUND))
            for h in range(MH):
                last = mm(ps[:, 4 + h // 2, (h % 2) * W1:(h % 2 + 1) * W1], kw[:, h, :], vm1[:, c, h, :], start=True, stop=True)
            last.then_inc(s("cup_done"), 1)

        def sample_inter(r):
            h, hf_ = r // 2, r % 2
            wait(pe, "st_done", r)
            pe.wait_ge(s(f"c_ld{hf_}"), 16 * (h + 1))
            wait(pe, "qg_done", 1)
            wait(pe, "cn_ready", r + 1)
            for j in range(4):
                c = inter_quarter(j, hf_)
                last = mm(ps[PQ * c:PQ * (c + 1), 4, IT0:IT0 + W1], qmT[:, h, T_P + PQ * hf_:T_P + PQ * (hf_ + 1)],
                          Cs[:, 4 * hf_ + j, :], start=True, stop=True, skip_group_check=True)
            last.then_inc(s("it_done"), 1)

        def sample_round(r):
            h, hf_ = r // 2, r % 2
            wait(pe, "st_done", r)
            wait(pe, "it_evac", r + 1)
            wait(pe, "kw_done", 1)
            wait(pe, "vmk_done", r + 1)
            for q in range(2):
                last = mm(ps[:, 4 + q, 0:2 * W1], kws[:, h, :], vmk[:, 2 * q:2 * q + 2, :].rearrange("p b v -> p (b v)"),
                          start=True, stop=True)
            last.then_inc(s("rcup_done"), 1)

        def h_transposes(u, it):
            _, _, n = unit_tokens(u)
            v = H_ORDER.index(u) + 1
            wait(pe, "h_done", v)
            wait(pe, "sd_done", min(it, NTILE))
            wait(pe, "hT_evac", v - 1)
            for h in range(MH):
                last = nc.tensor.transpose(ps[:, 1, h * n:(h + 1) * n], hs[0:n, h, :], ident[0:n, 0:n])
            last.then_inc(s("hT_done"), 1)

        for it in range(S_P4 - S_P3):
            if it <= NC:
                log_weights(it)
            if 3 <= it <= NC + 1:
                h_transposes(it - 2, it)
            if 2 <= it <= NC + 1:
                numerator(it - 1)
                state_update(it - 1)
            project(7)
            if it == NC + 2:
                h_transposes(NC, it)
                numerator(0)
            if it <= NC:
                m_scores(it)
            if 1 <= it <= N_ROUND:
                sample_inter(it - 1)
            project(7)
            if it == NC + 3:
                h_transposes(0, it)
            if 1 <= it <= N_ROUND:
                sample_round(it - 1)
            if it <= NC:
                k_transposes(it)
            project(10)

        project(24 * (NSUB - S_P4))

        def out_part(p, ks, qs=(0, 1)):
            t = Y_ORDER[p]
            off, n = x_cols(t)
            if t == NC:
                wait(pe, "os_ready", 2)
            for kk in ks:
                if p == 0:
                    wait(pe, "al_done" if kk < 4 else "ml_done", kk % 4 + 1)
                    wait(pe, "w_lo", POS[("out", kk)] + 1)
                hl, wh, wl = (a_hl, wah, wal) if kk < 4 else (m_hl, wbh, wbl)
                c0 = (kk % 4) * T + off
                for q in qs:
                    wc = slice(512 * q, 512 * (q + 1))
                    last = split_products(ps[:, 2 * (p % 4) + q, :], hl[:, :, c0:c0 + n], o_hl_s[:, kk], wh[:, kk % 4, wc], wl[:, kk % 4, wc],
                                          first=(kk == 0), final=(kk == KT - 1))
            if ks[-1] == KT - 1:
                last.then_inc(s("y_half" if qs == (0,) else "y_done"), 1)

        wait(pe, "hT_evac", NTILE)
        wait(pe, "h_done", NTILE)
        for p in range(4):
            if p == 3:
                wait(pe, "proj_free", NSUB)
            out_part(p, list(range(4)))
        for p in range(4):
            out_part(p, list(range(4, KT)))
        for p in range(4, NTILE):
            wait(pe, "y_free", p - 3)
            if p < NTILE - 1:
                out_part(p, list(range(KT)))
            else:
                out_part(p, list(range(KT)), (0,))
                out_part(p, list(range(KT)), (1,))

    @block.scalar
    def _(act):
        A_ = nc.scalar.activation

        def square(t):
            _, n = x_cols(t)
            act.wait_ge(s(f"x_ld{t % 4}"), 16 * (t // 4 + 1))
            wait(act, "ss_ready", t)
            A_(junk[0:n, :], x_raw[0:n, t % 4, :], ACT.Square, accum_out=stat[0:n, t:t + 1]).then_inc(s("ss_ready"), 1)

        def x_hi(t):
            off, n = x_cols(t)
            b = 2 * (t % 2)
            if t == 0:
                for q, event in enumerate(("xT_half", "xT_done")):
                    wait(act, event, 1)
                    A_(kx(xh, off, n)[:, 4 * q:4 * q + 4, :], ps[:, b + q, :].rearrange("p (k t) -> p k t", k=4), ACT.Copy)\
                        .then_inc(s("xh_ready" if q else "xh_half"), 1)
                return
            wait(act, "xT_done", t + 1)
            A_(kx(xh, off, n), bank_pair(b, P).rearrange("p b (k t) -> p (b k) t", k=4)[:, :, 0:n], ACT.Copy).then_inc(s("xh_ready"), 1)

        def token_evac(t):
            _, n = x_cols(t)
            b = 4 + 2 * (t % 2)
            wait(act, "tok_done", t + 1)
            if t == NC:
                act.wait_ge(s("ss_ready"), NTILE)
                A_(tok_lo[:], ps[n:2 * n, b:b + 2, 0:TOK_H], ACT.Copy).then_inc(s("tok_act"), 1)
                return
            A_(vm1[0:n, t, :, 0:MD].rearrange("p (b h) v -> p b h v", b=2),
               bank_pair(b, n, 2 * MD).rearrange("p b (h v) -> p b h v", h=2), ACT.Copy)
            A_(va[0:n, t, 0:VA0], ps[0:n, b, 2 * MD:TOK_H], ACT.Copy).then_inc(s("tok_act"), 1)

        def split_hi(n):
            kind, j = SEQ[n]
            if kind == "in":
                wait(act, "sub_done", 3 * (j - 1))
                dst = w_hi[:, j % 2, :]
            elif j < 4:
                if j == 0:
                    wait(act, "ag_done", G)
                    act.wait_ge(s("cp_st"), 32)
                    act.wait_ge(s("c_st0"), 16 * MH)
                    act.wait_ge(s("c_st1"), 16 * MH)
                dst = wah[:, j, :]
            else:
                wait(act, "sub_done", NSUB)
                dst = wbh[:, j - 4, :]
            act.wait_ge(s(f"w_ld{n % 2}"), 16 * (n // 2 + 1))
            A_(dst, w_raw[:, n % 2, :], ACT.Copy).then_inc(s("w_hi"), 1)

        def evac(sub):
            j, kind, t, off, w = sub_of(sub)
            cols = slice(off, off + w)
            wait(act, "sub_done", sub + 1)
            src = ps[:, 6 + sub % 2, 0:w]
            if kind in ("om", "zm"):
                m = sub - S_P4
                wait(act, "sg_used", m - 1)
                if m == 0:
                    wait(act, "hT_evac", NTILE)
                A_(sg[:, m % 2, 0:w], src, ACT.Sigmoid).then_inc(s("proj_free" if kind == "om" else "sgz_ready"), 1)
            else:
                if sub == 3 * FIRST["km"]:
                    act.wait_ge(s("m_out"), 16)
                    wait(act, "cols_ps", 1)
                if sub == S_P3:
                    act.wait_ge(s("k_outd"), 32)
                    wait(act, "pv_done", N_ATT)
                dst = {"ka": kaT[:, cols], "qa": qaT[:, t, cols], "km": kmT[:, t, cols], "qm": qmT[:, t, cols],
                       "za": zaT[:, t, cols]}[kind]
                A_(dst, src, ACT.Copy, scale=float(MD) ** -0.5 if kind == "km" else 1.0).then_inc(s("proj_free"), 1)
            for n in PLAN.get(sub, []):
                split_hi(n)

        def wt_hi_part(g):
            act.wait_ge(s(f"wt_ld{g}"), 16)
            r = slice(2 * g, 2 * g + 2)
            A_(wt_hi[:, r, :], wt_raw[:, r, :], ACT.Copy).then_inc(s("wt_hi_a"), 1)

        square(0)
        for t in range(NTILE):
            x_hi(t)
            if t == 0:
                square(1)
                wt_hi_part(2)
            if t + 2 < NTILE:
                square(t + 2)
            if t >= 2:
                token_evac(t - 2)
        token_evac(NTILE - 2)
        wait(act, "wt_split_d", 3)
        wait(act, "wt_split_p", 3)
        split_hi(0)
        token_evac(NTILE - 1)

        for sub in range(S_P2):
            evac(sub)
            if sub == 1:
                wait(act, "abs_f", 1)
                A_(rb[:], ra[:], ACT.Exp, scale=-1.0).then_inc(s("exp_f"), 1)
            if sub == 2:
                wait(act, "one_exp", 1)
                A_(rc[:], ra[:], ACT.Ln).then_inc(s("ln_f"), 1)
            if sub == 9:
                wait(act, "cols_dve", 1)
                for cs, n in COL_GROUPS:
                    last = A_(enm[0:n, cs, :], row_cols(2, cs, n), ACT.Exp, scale=-1.0)
                last.then_inc(s("cols_done"), 1)

        def exps(u):
            wait(act, "scored", u + 1)
            b = u % 2
            k0 = WIN if u < 2 else 0
            for g in range(4):
                p = prob[:, b, g, k0:] if u < 2 * NC else prob_s[:, g, :]
                A_(p, p, ACT.Exp, bias=nmx[:, b, g:g + 1], accum_out=den[:, b, g:g + 1])
            A_(sd[:, b, :], sd[:, b, :], ACT.Exp).then_inc(s("exp_done"), 1)

        def probT_evac(u):
            wait(act, "pTr_done", u + 1)
            wait(act, "pv_done", u - 1)
            n = P if u < 2 * NC else T_S
            A_(probT[0:n, u % 2, 1, :], ps[0:n, 3, :], ACT.Copy).then_inc(s("pT_act"), 1)

        def out_evac(u):
            wait(act, "pv_done", u + 1)
            if u < 2 * NC:
                blk, pair = u // 2, u % 2
                A_(qaT[:, 2 * pair:2 * pair + 2, blk * P:(blk + 1) * P],
                   ps[:, 4 + u % 2, 0:2 * P].rearrange("p (g t) -> p g t", g=2), ACT.Copy)\
                    .then_inc(s("att_out"), 1)
            else:
                A_(qaT[:, :, T_P:T].rearrange("p g (b t) -> p b g t", t=DEC_T),
                   ps[:, 4, 0:2 * P].rearrange("p (b g t) -> p b g t", g=G, t=DEC_T), ACT.Copy).then_inc(s("att_out"), 1)

        for it in range(S_P3 - S_P2):
            if 2 <= it <= N_ATT + 1:
                probT_evac(it - 2)
            if 3 <= it <= N_ATT + 2:
                out_evac(it - 3)
            if it < N_ATT:
                exps(it)
            if it == N_ATT + 2:
                wait(act, "ko_ps", 1)
                A_(k_out[:, 0, :], ps[:, 0, 0:P], ACT.Copy)
                A_(k_out[0:T_S, 1, :], ps[0:T_S, 0, P:2 * P], ACT.Copy).then_inc(s("ko_evac"), 1)
            evac(S_P2 + it)

        def g_exp(u):
            c, _, n = unit_tokens(u)
            wait(act, "r1_done", u + 1)
            wait(act, "st_done", u - 2)
            if u == 0:
                act.wait_ge(s("v_out"), 32)
                act.wait_ge(s("att_ld"), 64)
                A_(Gt[:, 0, 0:2, :].rearrange("p h t -> p (h t)"), ps[:, 0, 256:512], ACT.Exp).then_inc(s("g_done"), 1)
            else:
                if u == 2:
                    wait(act, "qg_done", 1)
                    wait(act, "dec_done", 1)
                for h in range(MH):
                    last = A_(Gt[:, u % 2, h, :], ps[:, 0, h * P:(h + 1) * P], ACT.Exp, bias=mpb[:, c, h:h + 1])
                last.then_inc(s("g_done"), 1)

        def d_exp(u):
            c, _, n = unit_tokens(u)
            wait(act, "mask_done", u + 1)
            for h in range(MH):
                last = A_(DT[0:n, h, 0:n], DT[0:n, h, 0:n], ACT.Exp, bias=r2c[0:n, c, h:h + 1])
            last.then_inc(s("d_done"), 1)

        def k_weight(u):
            _, _, n = unit_tokens(u)
            wait(act, "kT_done", u + 1)
            act.wait_ge(s("d_done"), u + 1)
            if u == 0:
                wait(act, "wss_done", 1)
            else:
                wait(act, "cup_done", u - 1)
            for h in range(MH):
                w = DT[:, h, P - 1:P] if u else wss[:, h:h + 1]
                last = A_((kw if u else kws)[0:n, h, :], ps[0:n, 0, h * P:(h + 1) * P], ACT.Copy, scale=w)
            last.then_inc(s("kw_done"), 1)

        def h_squares(u):
            _, _, n = unit_tokens(u)
            v = H_ORDER.index(u) + 1
            wait(act, "hden_done", v)
            wait(act, "hT_done", v - 1)
            wait(act, "hq_ready", v - 1)
            for h in range(MH):
                last = A_(hs[0:n, h, :], ps[0:n, 2 + h // 2, (h % 2) * W1:(h % 2) * W1 + MD], ACT.Square,
                          accum_out=hss[0:n, h:h + 1])
            last.then_inc(s("sq_done"), 1)

        for it in range(S_P4 - S_P3):
            if it <= NC:
                g_exp(it)
            if 2 <= it <= NC + 2:
                h_squares(it - 1 if it <= NC + 1 else 0)
            if 1 <= it <= N_ROUND and it % 2 == 1:
                wait(act, "it_done", it)
                A_(ITs[:, it // 2, :], ps[:, 4, IT0:IT0 + W1], ACT.Copy, scale=inter_msk[:, 0:1]).then_inc(s("it_evac"), 1)
            if it <= NC:
                d_exp(it)
            if it <= NC:
                k_weight(it)
            evac(S_P3 + it)

        def gate_a_sigmoid(t):
            if t == 0:
                wait(act, "hT_evac", NTILE)
                act.wait_ge(s("cp_st"), 32)
                act.wait_ge(s("c_st0"), 16 * MH)
                act.wait_ge(s("c_st1"), 16 * MH)
                wait(act, "proj_free", S_P4)
            wait(act, "za_used", t - 1)
            A_(sg_za[:, t % 2, :], zaT[:, t, :], ACT.Sigmoid).then_inc(s("sgza_ready"), 1)

        def a_hi(t):
            wait(act, "ag_done", t + 1)
            A_(ah[:, t * T:(t + 1) * T], qaT[:, t, :], ACT.Copy).then_inc(s("ah_done"), 1)

        for sub in range(S_P4, NSUB):
            m = sub - S_P4
            if m % 2 == 0 and m < 2 * G:
                gate_a_sigmoid(m // 2)
            if m % 2 == 1 and 3 <= m < 2 * G + 3:
                a_hi((m - 3) // 2)
            evac(sub)

        for j in range(MH):
            wait(act, "sg_used", 12 + 3 * (j + 1))
            wait(act, "sub_done", NSUB)
            A_(mh_[:, j * T:(j + 1) * T], qmT[:, j, :], ACT.Copy).then_inc(s("mh_done"), 1)
            split_hi(POS[("out", 4 + j)])
        SQ = dict(scale=float(D) ** -0.5)
        for p, t in enumerate(Y_ORDER):
            _, n = x_cols(t)
            b = 2 * (p % 4)
            wait(act, "ss_y", p)
            if p == NTILE - 1:
                for q, sums in enumerate((stat[:, p:p + 1], stat_2[:])):
                    wait(act, "y_done" if q else "y_half", NTILE if q else 1)
                    A_(junk5[:, 512 * q:512 * (q + 1)], ps[:, b + q, :], ACT.Square, accum_out=sums, **SQ).then_inc(s("ss_y"), 1)
                break
            wait(act, "y_done", p + 1)
            if t == NC:
                A_(y_lo[:], bank_pair(b, P)[n:2 * n].rearrange("p b c -> p (b c)"), ACT.Copy).then_inc(s("ylo_ready"), 1)
                wait(act, "y_sum", 1)
                y = y_out[0:n, p % 2, :]
            else:
                y = bank_pair(b, P).rearrange("p b c -> p (b c)")
            A_(junk5[0:n, :], y, ACT.Square, accum_out=stat[0:n, p:p + 1], **SQ).then_inc(s("ss_y"), 1)

    @block.vector
    def _(dve):
        V = nc.vector
        step = Step(dve, "dve_step")
        TT, TS, STT, CP = V.tensor_tensor, V.tensor_scalar, V.scalar_tensor_tensor, V.tensor_copy

        def x_norm(t):
            _, n = x_cols(t)
            wait(dve, "rstd_ready", t + 1)
            if t == 0:
                dve.wait_ge(s("gpre_ld"), 16)
            for cols in ([slice(0, 512), slice(512, D)] if t == 0 else [slice(0, D)]):
                x = x_raw[0:n, t % 4, cols]
                STT(out=x, in0=x, scalar=stat[0:n, NTILE + t:NTILE + t + 1], in1=g_pre_b[0:n, cols], op0=ALU.mult, op1=ALU.mult)\
                    .then_inc(s("xn_ready" if cols.stop == D else "xn_half"), 1)

        def x_lo(t):
            off, n = x_cols(t)
            b = 2 * (t % 2)
            if t == 0:
                for q, event in enumerate(("xh_half", "xh_ready")):
                    wait(dve, event, 1)
                    last = TT(kx(xl, off, n)[:, 4 * q:4 * q + 4, :], ps[:, b + q, :].rearrange("p (k t) -> p k t", k=4),
                              kx(xh, off, n)[:, 4 * q:4 * q + 4, :].bitcast(F32), ALU.subtract)
                last.then_inc(s("x_split"), 1)
                return
            wait(dve, "xh_ready", t + 1)
            TT(kx(xl, off, n), bank_pair(b, P).rearrange("p b (k t) -> p (b k) t", k=4)[:, :, 0:n],
               kx(xh, off, n).bitcast(F32), ALU.subtract).then_inc(s("x_split"), 1)
            if t == NC:
                dve.wait_ge(s("x_split"), NTILE)
                CP(x_hl_s[:].rearrange("p k a t -> p a k t"), x_hl[:].rearrange("p a (k t) -> p a k t", k=KT)[:, :, :, T_P:T])\
                    .then_inc(s("xs_ready"), 1)

        def wt_hi_part(g):
            dve.wait_ge(s(f"wt_ld{g}"), 16)
            r = slice(2 * g, 2 * g + 2)
            CP(wt_hi[:, r, :], wt_raw[:, r, :]).then_inc(s("wt_hi_d"), 1)

        def wt_lo_part(g):
            wait(dve, "wt_hi_d", [1, 2, 0, 3][g])
            r = slice(2 * g + (g == 0), 2 * g + 2)
            TT(wt_lo[:, r, :], wt_raw[:, r, :], wt_hi[:, r, :].bitcast(F32), ALU.subtract).then_inc(s("wt_split_d"), 1)

        def token_evac(t):
            _, n = x_cols(t)
            b = 4 + 2 * (t % 2)
            wait(dve, "tok_act", t + 1)
            if t == NC:
                def add(dst, q, c0, w):
                    return TT(dst, ps[0:n, b + q, c0:c0 + w], tok_lo[:, q, c0:c0 + w], ALU.add)
                add(va[0:n, t, 0:VA0], 0, 2 * MD, VA0)
                add(va[0:n, t, VA0:KV_W], 1, 2 * MD, KV_W - VA0)
                for q in range(2):
                    TT(vm1[0:n, t, 2 * q:2 * q + 2, 0:MD], ps[0:n, b + q, 0:2 * MD].rearrange("p (h v) -> p h v", h=2),
                       tok_lo[:, q, 0:2 * MD].rearrange("p (h v) -> p h v", h=2), ALU.add)
                    last = add(gates[0:n, t, q * PQ:q * PQ + MH], 1, TOK_H - 2 * MH + q * MH, MH)
                last.then_inc(s("tok_dve"), 1)
                return
            second = ps[0:n, b + 1, :]
            CP(va[0:n, t, VA0:KV_W], second[:, 2 * MD:2 * MD + KV_W - VA0])
            if t == 0:
                wait(dve, "gates_zero", 1)
            CP(gates[0:n, t, :].rearrange("p (q h) -> p q h", q=2)[:, :, 0:MH],
               second[:, TOK_H - 2 * MH:TOK_H].rearrange("p (q h) -> p q h", q=2)).then_inc(s("tok_dve"), 1)

        x_norm(0)
        wt_hi_part(0)
        x_lo(0)
        wt_lo_part(0)
        wt_hi_part(1)
        wt_lo_part(1)
        x_norm(1)
        wt_hi_part(3)
        wt_lo_part(3)
        x_lo(1)
        x_norm(2)
        for t in range(2, NTILE):
            if t + 1 < NTILE:
                x_norm(t + 1)
            x_lo(t)
            token_evac(t - 2)
        token_evac(NTILE - 2)
        token_evac(NTILE - 1)

        dve.wait_ge(s("misc_ld"), 16 * 13)
        dve.wait_ge(s("resets_ld"), 16)
        wait(dve, "rows_ps", 1)
        for dst, bias, q in ((ib, bgi, 0), (fb, bgf, PQ)):
            last = TS(dst[:], ps[q:q + MH, 0:3, :].rearrange("p b t -> p (b t)")[:, 0:T], bias[q:q + MH, 0:1], None, ALU.add)
        step(last)
        STT(out=ra[:], in0=fb[:], scalar=-1.0, in1=fb[:], op0=ALU.mult, op1=ALU.max).then_inc(s("abs_f"), 1)
        wait(dve, "exp_f", 1)
        wait(dve, "rows_zero", 1)
        step(TS(ra[:], rb[:], 1.0, None, ALU.add))
        STT(out=re_, in0=ra[:], scalar=1.0, in1=rb[:], op0=ALU.subtract, op1=ALU.subtract).then_inc(s("one_exp"), 1)
        wait(dve, "ln_f", 1)
        step(STT(out=rc[:], in0=fb[:], scalar=0.0, in1=rc[:], op0=ALU.min, op1=ALU.subtract))
        step(TT(rc[:], rc[:], re_, ALU.add))
        V.tensor_tensor_scan(out=ra[:], data0=resets[:], data1=rc[:], initial=0.0, op0=ALU.mult, op1=ALU.add)
        V.tensor_tensor_scan(out=rd[:, 0:T_P], data0=rc[:, 0:T_P], data1=ib[:, 0:T_P], initial=0.0, op0=ALU.add, op1=ALU.max)
        for b in range(DEC_B):
            c0 = T_P + DEC_T * b
            last = V.tensor_tensor_scan(out=rd[:, c0:c0 + DEC_T], data0=rc[:, c0:c0 + DEC_T], data1=ib[:, c0:c0 + DEC_T],
                                        initial=m0T[:, b:b + 1], op0=ALU.add, op1=ALU.max)
        step(last)
        CP(m_last[:, 0:1], rd[:, T_P - 1:T_P])
        CP(m_last[:, 1:1 + DEC_B], rd[:, T_P:T].rearrange("h (b t) -> h b t", t=DEC_T)[:, :, DEC_T - 1])
        V.memset(mp[:, 0:1], 0.0)
        CP(mp[:, 1:NC], rd[:, P - 1:T_P - P:P])
        step(CP(mp[:, NC:NC + DEC_B], m0T[:]))
        step(TT(re_, ra[:], rd[:], ALU.subtract))
        TT(rf, ib[:], ra[:], ALU.subtract)
        CP(r_m, rd[:])
        TT(r_gl[:, T_P:T].rearrange("h (b t) -> h b t", t=DEC_T), re_[:, T_P:T].rearrange("h (b t) -> h b t", t=DEC_T),
           mp[:, NC:NC + DEC_B].unsqueeze(2).broadcast_to([MH, DEC_B, DEC_T]), ALU.add)
        TT(mpd[:], mp[:, 0:NC].unsqueeze(2).broadcast_to([MH, NC, MH]),
           ident[0:MH, 0:MH].unsqueeze(1).broadcast_to([MH, NC, MH]), ALU.mult).then_inc(s("rows_done"), 1)
        wait(dve, "cols_ps", 1)
        for q, dst in enumerate((r1c, r2c)):
            for cs, n in COL_GROUPS:
                CP(dst[0:n, cs, :], row_cols(q, cs, n))
        CP(glc[:], row_cols(3, slice(NC, NTILE), T_S).rearrange("p c h -> p (c h)"))
        CP(mpb[:], ps[:, 2, 0:NC * MH].rearrange("p (c h) -> p c h", h=MH)).then_inc(s("cols_dve"), 1)

        def score(u):
            wait(dve, "qk_done", u + 1)
            wait(dve, "pTr_done", u - 1)
            b = u % 2
            if u == 0:
                dve.wait_ge(s("att_ld"), 64)
            if u < 2 * NC:
                heads = slice(4 * (u % 2), 4 * (u % 2) + 4)
                k0 = WIN if u < 2 else 0
                p = prob[:, b, :, k0:]
                step(STT(out=p, in0=ps[:, 0:2, :].rearrange("p b (g k) -> p (b g) k", g=2)[:, :, k0:], scalar=float(HD) ** -0.5,
                         in1=bias_p[:, heads, k0:], op0=ALU.mult, op1=ALU.add))
                sink = sink_p[:, heads]
            else:
                for kv in range(KVH):
                    last = STT(out=prob_s[:, 2 * kv:2 * kv + 2, :], in0=ps[:, kv, 0:2 * KEYS_S].rearrange("p (a k) -> p a k", a=2),
                               scalar=float(HD) ** -0.5, in1=bias_s[:, kv:kv + 1, :].broadcast_to([P, 2, KEYS_S]),
                               op0=ALU.mult, op1=ALU.add)
                step(last)
                p, sink = prob_s[:], sink_s[:]
            step(V.tensor_reduce(mx[:, b, :], p, AX_X, ALU.max))
            step(TT(mx[:, b, :], mx[:, b, :], sink, ALU.max))
            TS(nmx[:, b, :], mx[:, b, :], -1.0, None, ALU.mult)
            TT(sd[:, b, :], sink, mx[:, b, :], ALU.subtract).then_inc(s("scored"), 1)

        def denominators(u):
            b = u % 2
            wait(dve, "exp_done", u + 1)
            step(TT(den[:, b, :], den[:, b, :], sd[:, b, :], ALU.add))
            V.reciprocal(rden[:, b, :], den[:, b, :]).then_inc(s("rden_done"), 1)

        def probT_evac(u):
            wait(dve, "pTr_done", u + 1)
            wait(dve, "pv_done", u - 1)
            CP(probT[:, u % 2, 0, :], ps[:, 2, :]).then_inc(s("pT_dve"), 1)

        for it in range(S_P3 - S_P2):
            if 1 <= it <= N_ATT:
                denominators(it - 1)
            if 4 <= it <= N_ATT + 1:
                probT_evac(it - 2)
            if it == 2:
                CP(qs[:].rearrange("p b (g t) -> p b g t", g=G), qaT[:, :, T_P:T].rearrange("p g (b t) -> p b g t", t=DEC_T))
                CP(kcT[:, :, WIN:KEYS_S], kaT[:, T_P:T].rearrange("p (b t) -> p b t", t=DEC_T)).then_inc(s("qs_ready"), 1)
            if it < N_ATT:
                score(it)

        def sd_mul(u):
            _, _, n = unit_tokens(u)
            wait(dve, "d_done", u + 1)
            wait(dve, "s_done", u + 1)
            wait(dve, "num_done", u - 1)
            TT((SD if u else SDs)[0:n, :, :], ps[0:n, 1, 0:MH * n].rearrange("p (h t) -> p h t", h=MH), DT[0:n, :, 0:n], ALU.mult)\
                .then_inc(s("sd_done"), 1)

        def mask_weights(u):
            _, _, n = unit_tokens(u)
            wait(dve, "g_done", u + 1)
            wait(dve, "kw_done", u)
            m = causal if u else causal_s
            TT(DT[0:n, :, 0:n], ps[0:n, 0, 0:MH * n].rearrange("p (h t) -> p h t", h=MH),
               m[:].unsqueeze(1).broadcast_to([n, MH, n]), ALU.min).then_inc(s("mask_done"), 1)

        def q_gate(u):
            _, off, n = unit_tokens(u)
            wait(dve, "g_done", u + 1)
            wait(dve, "s_done", u + 1)
            g = Gt[:, u % 2, :, :] if u else Gt[:, 0, 0:2, :].rearrange("p a (h t) -> p (a h) t", t=T_S)
            q = qmT[:, :, off:off + n]
            TT(q, q, g, ALU.mult).then_inc(s("qg_done"), 1)

        def sample_extras():
            g = Gt[:, 0, 0:2, :].rearrange("p a (h b t) -> p (a h) b t", b=DEC_B, t=DEC_T)
            CP(dec_s[:].rearrange("p b h -> p h b"), g[:, :, :, DEC_T - 1]).then_inc(s("dec_done"), 1)
            V.tensor_reduce(wss[:], DT[0:T_S, :, DEC_T - 1:T_S:DEC_T], AX_X, ALU.add).then_inc(s("wss_done"), 1)

        def state(u):
            wait(dve, "cup_done", u)
            new = ps[:, 4:6, 0:2 * W1]
            if u == 1:
                CP(Cst[:].rearrange("p (b h) v -> p b (h v)", b=2), new).then_inc(s("st_done"), 1)
                return
            dve.wait_ge(s("st_done"), u - 1)
            for h in range(MH):
                last = STT(out=Cst[:, h, :], in0=Cst[:, h, :], scalar=Gt[:, u % 2, h, P - 1:P],
                           in1=ps[:, 4 + h // 2, (h % 2) * W1:(h % 2 + 1) * W1], op0=ALU.mult, op1=ALU.add)
            last.then_inc(s("st_done"), 1)
            if u == NC:
                dve.wait_ge(s("st_done"), NC)
                CP(n_p[:], Cst[:, :, MD]).then_inc(s("np_done"), 1)

        def sample_state(r):
            h, hf_ = r // 2, r % 2
            half_b = slice(4 * hf_, 4 * hf_ + 4)
            dve.wait_ge(s("cn_ready"), r + 1)
            wait(dve, "rcup_done", r + 1)
            for bb in range(4):
                b = 4 * hf_ + bb
                last = STT(out=Cs[:, b, :], in0=Cs[:, b, :], scalar=dec_s[:, b, h:h + 1],
                           in1=ps[:, 4 + bb // 2, (bb % 2) * W1:(bb % 2 + 1) * W1], op0=ALU.mult, op1=ALU.add)
            step(last)
            CP(n_s[:, half_b, h], Cs[:, half_b, MD]).then_inc(s("round_upd"), 1)

        def sample_n(r):
            bs = slice(4 * (r % 2), 4 * (r % 2) + 4)
            CP(Cs[:, bs, MD], n_s[:, bs, r // 2]).then_inc(s("cn_ready"), 1)

        def inter_second(r):
            wait(dve, "it_done", r + 1)
            wait(dve, "it_evac", r)
            part = ITs[:, r // 2, :]
            STT(out=part, in0=ps[:, 4, IT0:IT0 + W1], scalar=inter_msk[:, 1:2], in1=part, op0=ALU.mult, op1=ALU.add)\
                .then_inc(s("it_evac"), 1)

        def num_view(n):
            return ps[0:n, 2:4, 0:2 * W1].rearrange("p b (h v) -> p b h v", v=W1)

        def h_denominator(u):
            c, _, n = unit_tokens(u)
            v = H_ORDER.index(u) + 1
            wait(dve, "num_done", v)
            CP(hden[0:n, :].rearrange("p (b h) -> p b h", b=2), num_view(n)[:, :, :, MD]).then_inc(s("hden_done"), 1)
            dve.wait_ge(s("hden_done"), v)
            step(STT(out=hab[0:n, :], in0=hden[0:n, :], scalar=-1.0, in1=hden[0:n, :], op0=ALU.mult, op1=ALU.max))
            step(TT(hab[0:n, :], hab[0:n, :], enm[0:n, c, :], ALU.max))
            wait(dve, "hf_ready", v - 1)
            step(V.reciprocal(hrd[0:n, :], hab[0:n, :]))

        def h_mean_square(u):
            _, _, n = unit_tokens(u)
            v = H_ORDER.index(u) + 1
            wait(dve, "sq_done", v)
            wait(dve, "h_done", v - 1)
            step(STT(out=hf[0:n, :], in0=hss[0:n, :], scalar=1.0 / MD, in1=hrd[0:n, :], op0=ALU.mult, op1=ALU.mult))
            TT(hf[0:n, :], hf[0:n, :], hrd[0:n, :], ALU.mult).then_inc(s("hq_ready"), 1)

        def h_scale(u):
            _, _, n = unit_tokens(u)
            v = H_ORDER.index(u) + 1
            wait(dve, "hf_ready", v)
            TT(hs[0:n, :, :].rearrange("p (b h) v -> p b h v", b=2), num_view(n)[:, :, :, 0:MD],
               hf[0:n, :].rearrange("p (b h) -> p b h", b=2).unsqueeze(3).broadcast_to([n, 2, 2, MD]), ALU.mult)\
                .then_inc(s("h_done"), 1)

        def hT_evac(u):
            _, off, n = unit_tokens(u)
            v = H_ORDER.index(u) + 1
            wait(dve, "hT_done", v)
            TT(qmT[:, :, off:off + n], ps[:, 1, 0:MH * n].rearrange("p (h t) -> p h t", h=MH),
               gmh[:].unsqueeze(2).broadcast_to([P, MH, n]), ALU.mult).then_inc(s("hT_evac"), 1)

        def splits(sub):
            for n in PLAN.get(sub, []):
                split_lo(dve, V, n)

        for it in range(S_P4 - S_P3):
            if it >= 3:
                hT_evac(it - 2 if it <= NC + 2 else 0)
            done = None
            if 2 <= it <= NC + 2:
                done = it - 1 if it <= NC + 1 else 0
                h_denominator(done)
            if it <= NC:
                mask_weights(it)
            if 2 <= it <= NC + 1:
                state(it - 1)
            if 1 <= it <= N_ROUND and it % 2 == 0:
                inter_second(it - 1)
            if done is not None:
                h_mean_square(done)
                h_scale(done)
            if it <= NC:
                q_gate(it)
                sd_mul(it)
            if it == 0:
                sample_extras()
            if it >= 1:
                splits(S_P3 + it - 1)
            if 1 <= it <= N_ROUND:
                sample_state(it - 1)
            if it < N_ROUND:
                sample_n(it)

        def gate_a(t):
            wait(dve, "za_used", t + 1)
            TT(qaT[:, t, :], qaT[:, t, :], zaT[:, t, :], ALU.mult).then_inc(s("ag_done"), 1)

        def a_lo(t):
            wait(dve, "ah_done", t + 1)
            TT(al[:, t * T:(t + 1) * T], qaT[:, t, :], ah[:, t * T:(t + 1) * T].bitcast(F32), ALU.subtract).then_inc(s("al_done"), 1)

        for m in range(NSUB - S_P4):
            sub = S_P4 + m
            _, kind, _, _, w = sub_of(sub)
            splits(sub - 1)
            if m % 2 == 0 and m < 2 * G:
                gate_a(m // 2)
            if m % 2 == 1 and 3 <= m < 2 * G + 3:
                a_lo((m - 3) // 2)
            if kind == "zm":
                wait(dve, "sgz_ready", sub - 3 * FIRST["zm"] + 1)
                TT(sg[:, m % 2, 0:w], ps[:, 6 + sub % 2, 0:w], sg[:, m % 2, 0:w], ALU.mult).then_inc(s("proj_free"), 1)

        splits(NSUB - 1)
        for j in range(MH):
            split_lo(dve, V, POS[("out", 4 + j)])
            wait(dve, "mh_done", j + 1)
            TT(ml_[:, j * T:(j + 1) * T], qmT[:, j, :], mh_[:, j * T:(j + 1) * T].bitcast(F32), ALU.subtract)\
                .then_inc(s("ml_done"), 1)
        wait(dve, "al_done", G)
        dve.wait_ge(s("ml_done"), MH)
        for q, hl in enumerate((a_hl, m_hl)):
            CP(o_hl_s[:, 4 * q:4 * q + 4].rearrange("p k a t -> p a k t"),
               hl[:].rearrange("p a (k t) -> p a k t", k=MH)[:, :, :, T_P:T]).then_inc(s("os_ready"), 1)
        dve.wait_ge(s("gpost_ld"), 16)
        for p in range(NTILE - 1):
            t = Y_ORDER[p]
            _, n = x_cols(t)
            y = y_out[0:n, p % 2, :]
            src = bank_pair(2 * (p % 4), n).rearrange("p b c -> p (b c)")
            if p == 0:
                wait(dve, "sub_done", NSUB)
            if p >= 2:
                dve.wait_ge(s(f"y_st{p % 2}"), 16 * (p // 2))
            if t == NC:
                wait(dve, "ylo_ready", 1)
                TT(y, src, y_lo[:], ALU.add).then_inc(s("y_sum"), 1)
                wait(dve, "y_sum", 1)
                src = y
            wait(dve, "rs_y", p + 1)
            STT(out=y, in0=src, scalar=stat[0:n, NTILE + p:NTILE + p + 1], in1=g_post_b[0:n, :], op0=ALU.mult, op1=ALU.mult)\
                .then_inc(s("y_free"), 1)
            dve.wait_ge(s("y_free"), p + 1)
            dve.wait_ge(s(f"xr_ld{p % 2}"), 16 * (p // 2 + 1))
            TT(y, y, x_res[0:n, p % 2, :], ALU.add).then_inc(s("y_ready"), 1)
        p = NTILE - 1
        dve.wait_ge(s(f"y_st{p % 2}"), 16 * (p // 2))
        dve.wait_ge(s(f"xr_ld{p % 2}"), 16 * (p // 2 + 1))
        ys = [y_out[:, p % 2, 512 * q:512 * (q + 1)] for q in range(2)]
        for q in range(2):
            wait(dve, "ss_y", NTILE + q)
            TT(ys[q], ps[:, 2 * (p % 4) + q, :], g_post_b[:, 512 * q:512 * (q + 1)], ALU.mult).then_inc(s("yg_done"), 1)
        wait(dve, "rs_y", p + 1)
        for q in range(2):
            wait(dve, "yg_done", q + 1)
            STT(out=ys[q], in0=ys[q], scalar=stat[:, NTILE + p:NTILE + p + 1], in1=x_res[:, p % 2, 512 * q:512 * (q + 1)],
                op0=ALU.mult, op1=ALU.add).then_inc(s("y_ready"), 1)

    @block.gpsimd
    def _(pool):
        Q = nc.gpsimd
        step = Step(pool, "pool_step")

        def rsqrt(dst, mean_sq):
            n, w = mean_sq.shape
            return Q.tensor_tensor(dst, mean_sq, minus_half[0:n, 0:w], ALU.pow)

        step(Q.memset(minus_half[:], -0.5))
        Q.memset(ones[:], 1.0)
        Q.memset(vm1[:, :, :, MD:W1], 1.0).then_inc(s("ones_ready"), 1)

        Q.memset(gates[:], 0.0).then_inc(s("gates_zero"), 1)

        for t in range(NTILE):
            _, n = x_cols(t)
            wait(pool, "ss_ready", t + 1)
            r = stat[0:n, NTILE + t:NTILE + t + 1]
            step(Q.tensor_scalar(r, stat[0:n, t:t + 1], 1.0 / D, EPS, ALU.mult, ALU.add))
            rsqrt(r, r).then_inc(s("rstd_ready"), 1)
            for kk in [[0], [4, 5]][t] if t < 2 else []:
                wait(pool, ["wt_hi_d", "wt_hi_a"][t], 1)
                Q.tensor_tensor(wt_lo[:, kk, :], wt_raw[:, kk, :], wt_hi[:, kk, :].bitcast(F32), ALU.subtract)\
                    .then_inc(s("wt_split_p"), 1)

        split_lo(pool, Q, 0)
        wait(pool, "tok_done", NTILE)
        Q.memset(rows[:], 0.0).then_inc(s("rows_zero"), 1)

        def splits(sub):
            for n in PLAN.get(sub, []):
                split_lo(pool, Q, n)

        for sub in range(S_P2 - 1):
            splits(sub)

        def normalise(u):
            b = u % 2
            wait(pool, "rden_done", u + 1)
            if u < 2 * NC:
                k0 = WIN if u < 2 else 0
                p = prob[:, b, :, k0:]
                Q.tensor_tensor(p, p, rden[:, b, :].unsqueeze(2).broadcast_to([P, G, 2 * WIN - k0]), ALU.mult)\
                    .then_inc(s("prob_ready"), 1)
            else:
                step(Q.tensor_tensor(prob_s[:], prob_s[:], rden[:, b, :].unsqueeze(2).broadcast_to([P, 4, KEYS_S]), ALU.mult))
                for q in range(4):
                    last = Q.tensor_tensor(new_s[:, q, :].rearrange("p (b t) -> p b t", t=DEC_T),
                                           prob_s[:, q, WIN:KEYS_S].unsqueeze(1).broadcast_to([P, DEC_B, DEC_T]),
                                           newmask[:, q % 2, :].unsqueeze(2).broadcast_to([P, DEC_B, DEC_T]), ALU.mult)
                last.then_inc(s("prob_ready"), 1)

        for it in range(S_P3 - S_P2):
            if 1 <= it <= N_ATT:
                normalise(it - 1)
            splits(S_P2 + it - 1)

        def masked_values(r):
            h, hf_ = r // 2, r % 2
            wait(pool, "rcup_done", r)
            if r == 0:
                wait(pool, "g_done", 1)
                wait(pool, "scored", N_ATT)
            Q.tensor_tensor(vmk[:], vm1[0:T_S, NC, h:h + 1, :].broadcast_to([T_S, 4, W1]),
                            seqsel[:, 4 * hf_:4 * hf_ + 4].unsqueeze(2).broadcast_to([T_S, 4, W1]), ALU.mult)\
                .then_inc(s("vmk_done"), 1)

        def h_factor(u):
            _, _, n = unit_tokens(u)
            v = H_ORDER.index(u) + 1
            wait(pool, "hq_ready", v)
            step(Q.tensor_scalar(hf[0:n, :], hf[0:n, :], EPS, None, ALU.add))
            step(rsqrt(hf[0:n, :], hf[0:n, :]))
            Q.tensor_tensor(hf[0:n, :], hf[0:n, :], hrd[0:n, :], ALU.mult).then_inc(s("hf_ready"), 1)

        for it in range(S_P4 - S_P3):
            if 2 <= it <= NC + 2:
                h_factor(it - 1 if it <= NC + 1 else 0)
            if it < N_ROUND:
                masked_values(it)

        for m in range(NSUB - S_P4):
            sub = S_P4 + m
            _, kind, t, off, w = sub_of(sub)
            if m % 2 == 0 and m < 2 * G:
                q = m // 2
                wait(pool, "sgza_ready", q + 1)
                Q.tensor_tensor(zaT[:, q, :], zaT[:, q, :], sg_za[:, q % 2, :], ALU.mult).then_inc(s("za_used"), 1)
            wait(pool, "proj_free", sub + 1)
            x = qmT[:, t, off:off + w]
            Q.tensor_tensor(x, x, sg[:, m % 2, 0:w], ALU.mult).then_inc(s("sg_used"), 1)

        for p, t in enumerate(Y_ORDER):
            _, n = x_cols(t)
            wait(pool, "ss_y", p + 1)
            r = stat[0:n, NTILE + p:NTILE + p + 1]
            step(Q.tensor_scalar(r, stat[0:n, p:p + 1], 1.0, EPS, ALU.mult, ALU.add))
            if p == NTILE - 1:
                wait(pool, "ss_y", p + 2)
                step(Q.tensor_tensor(r, r, stat_2[0:n, :], ALU.add))
            rsqrt(r, r).then_inc(s("rs_y"), 1)

    block.__exit__(None, None, None)


OUTPUTS = [("y_prompt", (1, T_P, D)), ("y_sample", (DEC_B, DEC_T, D)),
           ("win_k_prompt", (1, 1, WIN, KVH, HD)), ("win_v_prompt", (1, 1, WIN, KVH, HD)),
           ("C_prompt", (1, 1, MH, MD, MD)), ("n_prompt_T", (MD, MH)), ("m_last_T", (MH, 1 + DEC_B)),
           ("win_k_sample", (1, DEC_B, WIN, KVH, HD)), ("win_v_sample", (1, DEC_B, WIN, KVH, HD)),
           ("C_sample", (1, DEC_B, MH, MD, MD)), ("n_sample_T", (MD, DEC_B, MH))]


def constants():
    f = np.float32
    tok = np.arange(P)
    slopes = (2.0 ** (-8.0 * (np.arange(AH) + 1) / AH)).astype(f)

    def bias(diff, slope):
        return np.where((diff >= 0) & (diff < WIN), -slope * diff.astype(f), f(NEG)).astype(f)

    diff = tok[:, None, None] + WIN - np.arange(2 * WIN)[None, None, :]
    bias_prompt = bias(diff, slopes[None, UNIT_HEADS, None])
    g, t = (tok // DEC_T) % G, tok % DEC_T
    bias_sample = np.stack([bias(t[:, None] + WIN - np.arange(KEYS_S)[None, :], slopes[kv * G + g][:, None])
                            for kv in range(KVH)], axis=1)
    st = np.arange(T_S)
    same = st[:, None] // DEC_T == st[None, :] // DEC_T
    resets = np.ones((MH, T), f)
    resets[:, 0:T_P:P] = 0
    resets[:, T_P::DEC_T] = 0
    own = np.arange(DEC_B)[None, None, :] == 4 * np.arange(2)[None, :, None] + (tok // 32)[:, None, None]
    inter = np.zeros((2, P, T_S), f)
    for hf in range(2):
        for j in range(4):
            for t in range(DEC_T):
                inter[hf, PQ * inter_quarter(j, hf) + DEC_T * j + t, PQ * hf + DEC_T * j + t] = 1
    return {"ident": np.eye(P, dtype=f), "inter_mask": inter.max(2).T, "inter_select": inter.sum(0),
            "chunk_mask": np.where(tok[:, None] > tok[None, :], f(NEG), f(-NEG)),
            "seq_mask": np.where(same & (st[:, None] <= st[None, :]), f(-NEG), f(NEG)),
            "bias_prompt": bias_prompt, "bias_sample": bias_sample, "resets": resets,
            "new_key_mask": own.astype(f),
            "seq_select": (st[:, None] // DEC_T == np.arange(DEC_B)[None, :]).astype(f)}


def kernel(**inputs):
    import concourse.bacc as bacc
    from concourse.bass_utils import run_bass_kernel_spmd

    a = {n: np.asarray(v) for n, v in inputs.items()}
    w_in, w_out = a["w_in"][0], a["w_out"][0]

    def pair_heads(off):
        cols = np.arange(AH * HD).reshape(KVH, G, HD).transpose(1, 0, 2).reshape(G, P)
        return [off + c for c in cols]

    tile_cols = [np.arange(C_KA, C_KA + KV_W)] + pair_heads(C_QA)
    for off in (C_KM, C_QM):
        tile_cols += [np.arange(off + P * t, off + P * (t + 1)) for t in range(MH)]
    tile_cols += pair_heads(C_ZA)
    for off in (C_OM, C_ZM):
        tile_cols += [np.arange(off + P * t, off + P * (t + 1)) for t in range(MH)]
    rows = w_in.reshape(KT, P, -1)
    w_in_tiles = np.stack([rows[:, :, c].transpose(1, 0, 2).reshape(P, KT * P) for c in tile_cols])
    tok_cols = np.concatenate([np.arange(C_VM, C_VM + 2 * MD), np.arange(C_VA, C_VA + VA0),
                               np.arange(C_VM + 2 * MD, C_VM + 4 * MD), np.arange(C_VA + VA0, C_VA + KV_W),
                               np.arange(C_G, C_G + 2 * MH)])
    w_tok = rows[:, :, tok_cols].transpose(1, 0, 2)
    w_out_tiles = np.concatenate([np.stack([w_out[c] for c in pair_heads(0)]), w_out[A_W:].reshape(MH, P, D)])
    sinks = a["attn_sinks"].reshape(KVH, G)
    rows_g = (np.arange(P) // DEC_T) % G
    arrays = {
        "x_prompt": a["x_prompt"], "x_sample": a["x_sample"], "g_pre": a["g_pre"], "g_post": a["g_post"],
        "w_tok": w_tok, "w_in_tiles": w_in_tiles, "w_out_tiles": w_out_tiles,
        "cache_win_k": a["cache_win_k"], "cache_win_v": a["cache_win_v"],
        "cache_k_T": a["cache_win_k"][0].transpose(2, 3, 0, 1).reshape(P, DEC_B, WIN),
        "state_C": a["state_C"], "state_n_T": a["state_n"][0].transpose(2, 0, 1), "state_m_T": a["state_m"][0].T,
        "b_gate": a["b_gate"].reshape(2 * MH, 1), "g_mh_T": a["g_mh"][0].T,
        "sinks_prompt": np.broadcast_to(a["attn_sinks"].reshape(AH)[UNIT_HEADS], (P, AH)),
        "sinks_sample": np.stack([sinks[q // 2][rows_g] for q in range(4)], axis=1),
        **constants(),
    }
    arrays = {n: np.ascontiguousarray(v) for n, v in arrays.items()}
    nc = bacc.Bacc("TRN2", target_bir_lowering=False, num_devices=1)
    ins = {n: nc.dram_tensor(f"in_{n}", v.shape, mybir.dt.from_np(v.dtype), kind="ExternalInput").ap()
           for n, v in arrays.items()}
    outs = {n: nc.dram_tensor(f"out_{n}", shape, F32, kind="ExternalOutput").ap() for n, shape in OUTPUTS}
    build(nc, ins, outs)
    r = run_bass_kernel_spmd(nc, [{f"in_{n}": v for n, v in arrays.items()}], core_ids=[0]).results[0]
    got = {n: np.asarray(r[f"out_{n}"]) for n, _ in OUTPUTS}
    got["n_prompt_T"] = np.ascontiguousarray(got["n_prompt_T"].T).reshape(1, 1, MH, MD)
    got["n_sample_T"] = np.ascontiguousarray(got["n_sample_T"].transpose(1, 2, 0)).reshape(1, DEC_B, MH, MD)
    m_last = got["m_last_T"]
    got["m_last_T"] = np.ascontiguousarray(m_last[:, 0]).reshape(1, 1, MH)
    return tuple(got[n] for n, _ in OUTPUTS) + (np.ascontiguousarray(m_last[:, 1:].T).reshape(1, DEC_B, MH),)
```
